# Optimizing a Trainium2 kernel written in Bass

```python
import jax, jax.numpy as jnp
from jax import lax
import numpy as np

D_MODEL = 1024
BATCH = 1
SEQ = 1024
DEPTH = 2

GRID_W = 64
CTX_LEN = 256
N_MIXERS = 2
D_INNER = D_MODEL
HEAD_DIM = 64
N_HEADS = D_INNER // HEAD_DIM
N_FGROUPS = 8
FGROUP_DIM = D_INNER // N_FGROUPS
LORA_DECAY = 64
LORA_ICLR = 64
LORA_VRES = 32
N_DIR = 2
N_TSHIFT = 6
N_FOURIER = (DEPTH + 1) // 2
N_RWKV = DEPTH // 2
RMS_EPS = 1e-6
GN_EPS = 64e-5

kernel_name = "fnet_rwkv7_sandwich_adaln_prefix_trunk"

def rmsnorm(x, g):
    x32 = x.astype(jnp.float32)
    y = x32 * lax.rsqrt(jnp.mean(x32 * x32, axis=-1, keepdims=True) + RMS_EPS)
    return (y * g.astype(jnp.float32)).astype(x.dtype)

def modulation(cond, w, b):
    return jnp.split(jax.nn.silu(cond) @ w + b, 3, axis=-1)

def shift_grid(h):
    b_, t, d = h.shape
    g = h.reshape(b_, t // GRID_W, GRID_W, d)
    p = jnp.pad(g, ((0, 0), (1, 1), (1, 1), (0, 0)))
    nb = (p[:, :-2, 1:-1] + p[:, 2:, 1:-1] + p[:, 1:-1, :-2] + p[:, 1:-1, 2:]) * 0.25
    return nb.reshape(b_, t, d)

def shift_seq(h):
    p = jnp.pad(h, ((0, 0), (1, 1), (0, 0)))
    return (p[:, :-2] + p[:, 2:]) * 0.5

def fourier_mixer(h, w_in, w_mix, b_mix, w_out):
    b_, t, _ = h.shape
    u, z = jnp.split(h @ w_in, 2, axis=-1)
    ug = u.reshape(b_, t, N_FGROUPS, FGROUP_DIM).astype(jnp.float32)
    f = jnp.fft.fftn(ug, axes=(1, 3), norm="ortho").real.astype(h.dtype)
    f = jnp.einsum('btgc,gce->btge', f, w_mix).reshape(b_, t, D_INNER) + b_mix
    return (f * jax.nn.silu(z)) @ w_out

def rwkv_features(h, shift_fn, mu, w_in, w0, w1, w2, a0, a1, a2, k_k, k_a, v_res):
    heads = lambda t: t.reshape(t.shape[:-1] + (N_HEADS, HEAD_DIM))
    xs = h[None] + (shift_fn(h) - h)[None] * mu[:, None, None, :]
    r, k, v, gz = jnp.einsum('pbtd,pde->pbte', xs[:4], w_in)
    xv, xw, xa = xs[2], xs[4], xs[5]
    if v_res is not None:
        v_first, v0, v1, v2 = v_res
        v = v + (v_first - v) * jax.nn.sigmoid(v0 + (xv @ v1) @ v2)
    kk = heads(k * k_k).astype(jnp.float32)
    kk = kk / jnp.maximum(jnp.linalg.norm(kk, axis=-1, keepdims=True), 1e-12)
    wz = w0[:, None, None, :] + jnp.einsum('nbtl,nle->nbte', jnp.tanh(jnp.einsum('btd,ndl->nbtl', xw, w1)), w2)
    decay = jnp.exp(-jnp.exp(-jax.nn.softplus(-wz.astype(jnp.float32)) - 0.5))
    a = jax.nn.sigmoid(a0[:, None, None, :] + jnp.einsum('nbtl,nle->nbte', jnp.einsum('btd,ndl->nbtl', xa, a1), a2))
    k_dir = k[None] * (1 + (a - 1) * k_a)
    b = kk[None] * heads(a)
    return heads(r), heads(k_dir), heads(v), kk, heads(decay), b, gz, v

def wkv_scan(state, r, w, k, v, a, b, reverse):
    def step(s, inp):
        r_t, w_t, k_t, v_t, a_t, b_t = inp
        sa = jnp.einsum('bhij,bhj->bhi', s, a_t)
        s = s * w_t[:, :, None, :] + sa[..., None] * b_t[:, :, None, :] + v_t[..., None] * k_t[:, :, None, :]
        return s, jnp.einsum('bhij,bhj->bhi', s, r_t)
    tm = lambda t: jnp.swapaxes(t, 0, 1).astype(jnp.float32)
    state, y = lax.scan(step, state, tuple(tm(t) for t in (r, w, k, v, a, b)), reverse=reverse)
    return state, jnp.swapaxes(y, 0, 1)

def run_scan(state, feats, n, reverse):
    r, k_dir, v, kk, decay, b = feats[:6]
    return wkv_scan(state, r, decay[n], k_dir[n], v, -kk, b[n], reverse)

def rwkv_output(y, feats, r_k, ln_w, ln_b, w_out):
    r, k_dir, v, gz = feats[0], feats[1], feats[2], feats[6]
    b_, t = y.shape[:2]
    mean = jnp.mean(y, axis=-1, keepdims=True)
    var = jnp.mean(jnp.square(y - mean), axis=-1, keepdims=True)
    yn = ((y - mean) * lax.rsqrt(var + GN_EPS)).reshape(b_, t, D_INNER).astype(gz.dtype) * ln_w + ln_b
    bonus = jnp.sum(jnp.sum(r[None] * k_dir * r_k, axis=-1, keepdims=True), axis=0) * v
    return ((yn + bonus.reshape(b_, t, D_INNER)) * jax.nn.silu(gz)) @ w_out

def rwkv_mixer(h_ctx, h_lat, mu, w_in, w0, w1, w2, a0, a1, a2, k_k, k_a, r_k, ln_w, ln_b, w_out,
               v_res_ctx, v_res_lat, ctx_out):
    fc = rwkv_features(h_ctx, shift_seq, mu, w_in, w0, w1, w2, a0, a1, a2, k_k, k_a, v_res_ctx)
    fl = rwkv_features(h_lat, shift_grid, mu, w_in, w0, w1, w2, a0, a1, a2, k_k, k_a, v_res_lat)
    state0 = jnp.zeros((h_lat.shape[0], N_HEADS, HEAD_DIM, HEAD_DIM), jnp.float32)
    y_ctx = 0.0
    y_lat = 0.0
    for n, rev in enumerate((False, True)):
        s_ctx, yc = run_scan(state0, fc, n, rev)
        _, yl = run_scan(s_ctx, fl, n, rev)
        y_ctx = y_ctx + yc
        y_lat = y_lat + yl
    out_lat = rwkv_output(y_lat, fl, r_k, ln_w, ln_b, w_out)
    out_ctx = rwkv_output(y_ctx, fc, r_k, ln_w, ln_b, w_out) if ctx_out else None
    return out_ctx, out_lat, fc[7], fl[7]

def setup_inputs(seed: int = 0) -> dict:
    key = jax.random.key(seed)
    ks = iter(jax.random.split(key, 40))
    nrm = lambda shape, s: jax.random.normal(next(ks), shape, jnp.float32) * s
    nv = max(N_RWKV - 1, 0)
    return {
        "x": nrm((BATCH, SEQ, D_MODEL), 1.0),
        "c": nrm((BATCH, D_MODEL), 1.0),
        "ctx": nrm((BATCH, CTX_LEN, D_MODEL), 1.0),
        "c_ctx": nrm((D_MODEL,), 1.0),
        "mod_w": nrm((DEPTH, D_MODEL, 3 * D_MODEL), D_MODEL ** -0.5),
        "mod_b": nrm((DEPTH, 3 * D_MODEL), 0.02),
        "norm_pre": 1.0 + nrm((DEPTH, D_MODEL), 0.05),
        "norm_post": 1.0 + nrm((DEPTH, D_MODEL), 0.05),
        "f_w_in": nrm((N_FOURIER, D_MODEL, 2 * D_INNER), D_MODEL ** -0.5),
        "f_w_mix": nrm((N_FOURIER, N_FGROUPS, FGROUP_DIM, FGROUP_DIM), FGROUP_DIM ** -0.5),
        "f_b_mix": nrm((N_FOURIER, D_INNER), 0.02),
        "f_w_out": nrm((N_FOURIER, D_INNER, D_MODEL), D_INNER ** -0.5),
        "r_mu": jax.random.uniform(next(ks), (N_RWKV, N_TSHIFT, D_MODEL), jnp.float32),
        "r_w_in": nrm((N_RWKV, 4, D_MODEL, D_INNER), D_MODEL ** -0.5),
        "r_w0": jax.random.uniform(next(ks), (N_RWKV, N_DIR, D_INNER), jnp.float32, minval=-3.0, maxval=0.5),
        "r_w1": nrm((N_RWKV, N_DIR, D_MODEL, LORA_DECAY), D_MODEL ** -0.5),
        "r_w2": nrm((N_RWKV, N_DIR, LORA_DECAY, D_INNER), 0.5 * LORA_DECAY ** -0.5),
        "r_a0": nrm((N_RWKV, N_DIR, D_INNER), 0.5),
        "r_a1": nrm((N_RWKV, N_DIR, D_MODEL, LORA_ICLR), D_MODEL ** -0.5),
        "r_a2": nrm((N_RWKV, N_DIR, LORA_ICLR, D_INNER), LORA_ICLR ** -0.5),
        "r_v0": nrm((nv, D_INNER), 0.5),
        "r_v1": nrm((nv, D_MODEL, LORA_VRES), D_MODEL ** -0.5),
        "r_v2": nrm((nv, LORA_VRES, D_INNER), LORA_VRES ** -0.5),
        "r_k_k": 1.0 + nrm((N_RWKV, D_INNER), 0.1),
        "r_k_a": 1.0 + nrm((N_RWKV, D_INNER), 0.1),
        "r_r_k": nrm((N_RWKV, N_HEADS, HEAD_DIM), 0.1),
        "r_ln_w": 1.0 + nrm((N_RWKV, D_INNER), 0.05),
        "r_ln_b": nrm((N_RWKV, D_INNER), 0.01),
        "r_w_out": nrm((N_RWKV, D_INNER, D_MODEL), D_INNER ** -0.5),
    }

def reference(x, c, ctx, c_ctx, mod_w, mod_b, norm_pre, norm_post, f_w_in, f_w_mix, f_b_mix, f_w_out,
              r_mu, r_w_in, r_w0, r_w1, r_w2, r_a0, r_a1, r_a2, r_v0, r_v1, r_v2,
              r_k_k, r_k_a, r_r_k, r_ln_w, r_ln_b, r_w_out):
    cond_lat = c[:, None, :]
    cond_ctx = c_ctx[None, None, :]
    v_first_ctx = None
    v_first_lat = None
    for i in range(DEPTH):
        last = i == DEPTH - 1
        kind = i % N_MIXERS
        j = i // N_MIXERS
        need_ctx = (not last) or kind == 1
        sh, sc, gt = modulation(cond_lat, mod_w[i], mod_b[i])
        h_lat = rmsnorm(x, norm_pre[i]) * (1 + sc) + sh
        if need_ctx:
            sh_c, sc_c, gt_c = modulation(cond_ctx, mod_w[i], mod_b[i])
            h_ctx = rmsnorm(ctx, norm_pre[i]) * (1 + sc_c) + sh_c
        if kind == 0:
            o_lat = fourier_mixer(h_lat, f_w_in[j], f_w_mix[j], f_b_mix[j], f_w_out[j])
            o_ctx = None if last else fourier_mixer(h_ctx, f_w_in[j], f_w_mix[j], f_b_mix[j], f_w_out[j])
        else:
            if j == 0:
                vres_c = None
                vres_l = None
            else:
                vres_c = (v_first_ctx, r_v0[j - 1], r_v1[j - 1], r_v2[j - 1])
                vres_l = (v_first_lat, r_v0[j - 1], r_v1[j - 1], r_v2[j - 1])
            o_ctx, o_lat, v_c, v_l = rwkv_mixer(
                h_ctx, h_lat, r_mu[j], r_w_in[j], r_w0[j], r_w1[j], r_w2[j], r_a0[j], r_a1[j], r_a2[j],
                r_k_k[j], r_k_a[j], r_r_k[j], r_ln_w[j], r_ln_b[j], r_w_out[j], vres_c, vres_l, not last)
            if j == 0:
                v_first_ctx = v_c
                v_first_lat = v_l
        x = x + gt * rmsnorm(o_lat, norm_post[i])
        if not last:
            ctx = ctx + gt_c * rmsnorm(o_ctx, norm_post[i])
    return x


_drawn_inputs = setup_inputs


def setup_inputs(seed=0):
    import zlib

    import numpy as np

    out = dict(_drawn_inputs(seed))
    spreads = {}
    factors = {'f_b_mix': 3.676, 'r_ln_w': 2.852, 'r_ln_b': 40.768}
    for name, (base, spread) in spreads.items():
        noise = np.random.default_rng([zlib.crc32(name.encode()), seed]).standard_normal(out[name].shape)
        drawn = base * np.exp(spread * noise) if base else spread * noise
        out[name] = __import__('jax').numpy.asarray(drawn.astype(out[name].dtype))
    for name, factor in factors.items():
        out[name] = (out[name] * factor).astype(out[name].dtype)
    return out
```

```python
from contextlib import ExitStack

import numpy as np

import concourse.bass as bass
from concourse import mybir

F32 = mybir.dt.float32
I32 = mybir.dt.int32
ALU = mybir.AluOpType
ACT = mybir.ActivationFunctionType

P = 128
D = 1024
KT = D // P
CTX = 256
LAT = 1024
T = CTX + LAT
HD = 64
LORA = 64
NDIR = 2
CH = 128
NCH = T // CH
NCC = NCH // 2
FG = P
HALF = LAT // 2
BLK = [(0, 512), (512, 512), (1024, 256)]
RMS_EPS = 1e-6
GN_EPS = 64e-5
DECAY = float(np.exp(-0.5))
SHIFT = DECAY * CH / 2

VEC = {}
for _n, _k in (("c", 1), ("c_ctx", 1), ("mod_b0", 3), ("mod_b1", 3), ("norm_pre", 2), ("norm_post", 2),
               ("f_b_mix", 1), ("mu", 6), ("w0", 2), ("a0", 2), ("k_k", 1), ("k_a", 1), ("r_k", 1),
               ("ln_w", 1), ("ln_b", 1)):
    VEC[_n] = sum(v[1] for v in VEC.values()) if VEC else 0
    VEC[_n] = (VEC[_n], _k * KT)
NVEC = sum(v[1] for v in VEC.values())

FEATS = ("kd", "b", "negkk", "r", "v", "sw")
NF = len(FEATS)


def lat(a):
    return slice(CTX + a, CTX + LAT)


def build(nc, A):
    es = ExitStack()
    with es:
        def sem(name):
            return es.enter_context(nc.semaphore(name))

        def dram(name, shape):
            return nc.dram_tensor(name, shape, F32, kind="Internal").ap()

        x1_d = dram("x1_scratch", [P, KT, LAT])
        sa_d = dram("iclr_scratch", [KT, P, NDIR, T])
        ks_d = dram("ksum_scratch", [KT, P, LAT])
        bv_d = dram("bonus_scratch", [KT, P, LAT])
        gz_d = dram("gate_scratch", [KT, P, LAT])
        fe_d = dram("feature_scratch", [KT * NCH, P, NF, NDIR, CH])
        y_d = dram("y_scratch", [KT * NCH, P, NDIR, CH])
        fe_v = fe_d.rearrange("(j c) p f d t -> j p f d c t", c=NCH)
        y_v = y_d.rearrange("(j c) p d t -> j p d c t", c=NCH)

        ps = es.enter_context(nc.psum_tensor("ps", [P, 8, 512], F32))
        vec = es.enter_context(nc.sbuf_tensor("vec", [P, NVEC], F32))
        mod = es.enter_context(nc.sbuf_tensor("mod", [P, 2, 24, 2], F32))
        pre_s = es.enter_context(nc.sbuf_tensor("pre_s", [P, 2, KT, 2], F32))
        post_s = es.enter_context(nc.sbuf_tensor("post_s", [P, 2, KT, 2], F32))
        ones = es.enter_context(nc.sbuf_tensor("ones", [P, P], F32))
        hones = es.enter_context(nc.sbuf_tensor("hones", [P, P], F32))
        ident = es.enter_context(nc.sbuf_tensor("ident", [P, P], F32))
        eps = es.enter_context(nc.sbuf_tensor("eps", [P, 4], F32))
        kam = es.enter_context(nc.sbuf_tensor("kam", [P, KT], F32))
        nkk = es.enter_context(nc.sbuf_tensor("nkk", [P, KT], F32))
        const_ready = sem("const_ready")

        def vcol(name, i, n=1):
            return vec[:, bass.ds(VEC[name][0] + i, n)]

        with ExitStack() as ph:
            wm = ph.enter_context(nc.sbuf_tensor("mod_slab", [P, 4, KT, P], F32))
            cond = ph.enter_context(nc.sbuf_tensor("cond", [P, KT, 2], F32))
            sig = ph.enter_context(nc.sbuf_tensor("cond_sig", [P, 2 * KT], F32))
            vec_in, slab_in = sem("vec_in"), [sem(f"mod_slab_in{i}") for i in range(4)]
            cond_ready, mod_mm, mod_out, cst, vchain = sem("cond_ready"), sem("mod_mm"), sem("mod_out"), sem("cst"), sem("mod_chain")
            cond_sig = sem("cond_sig_ready")
            NS = 48
            with nc.Block() as block:
                @block.sync
                def _(sp):
                    sp.dma_start(vec[:], A["vec"]).then_inc(vec_in, 16)
                    for s in range(4):
                        sp.dma_start(wm[:, s], A["modw"][s]).then_inc(slab_in[s], 16)
                    with sp.Fori(1, NS // 4) as i:
                        for s in range(4):
                            sp.wait_ge(mod_mm, i * 4 + (s - 3))
                            sp.dma_start(wm[:, s], A["modw"][i * 4 + s]).then_inc(slab_in[s], 16)

                @block.gpsimd
                def _(g):
                    g.memset(ones[:], 1.0).then_inc(cst, 1)
                    g.memset(ident[:], 0.0).then_inc(cst, 1)
                    g.memset(hones[:], 0.0).then_inc(cst, 1)
                    g.memset(eps[:, 0:1], RMS_EPS).then_inc(cst, 1)
                    g.memset(eps[:, 1:2], GN_EPS).then_inc(cst, 1)
                    g.memset(eps[:, 2:3], SHIFT).then_inc(cst, 1)
                    g.memset(eps[:, 3:4], -SHIFT).then_inc(cst, 1)
                    g.wait_ge(cst, 7)
                    g.affine_select(out=ident[:], in_=ident[:], compare_op=ALU.not_equal, fill=1.0, base=0,
                                    pattern=[[-1, P]], channel_multiplier=1).then_inc(cst, 1)
                    g.wait_ge(cst, 8)
                    g.memset(hones[0:HD, 0:HD], 1.0).then_inc(cst, 1)
                    g.wait_ge(cst, 9)
                    g.memset(hones[HD:P, HD:P], 1.0).then_inc(cst, 1)

                @block.scalar
                def _(act):
                    act.wait_ge(vec_in, 16)
                    act.activation(sig[:], vec[:, 0:2 * KT], ACT.Sigmoid).then_inc(cond_sig, 1)

                @block.vector
                def _(v):
                    n = [0]

                    def link(ins):
                        n[0] += 1
                        ins.then_inc(vchain, 1)
                        v.wait_ge(vchain, n[0])

                    v.wait_ge(vec_in, 16)
                    link(v.tensor_scalar(kam[:], vcol("k_a", 0, KT), -1.0, 1.0, ALU.mult, ALU.add))
                    link(v.tensor_scalar(nkk[:], vcol("k_k", 0, KT), -1.0, None, ALU.mult))
                    v.wait_ge(cond_sig, 1)
                    v.tensor_tensor(cond[:].rearrange("p k c -> p c k"), vec[:, 0:2 * KT].rearrange("p (c k) -> p c k", c=2),
                                    sig[:].rearrange("p (c k) -> p c k", c=2), ALU.mult).then_inc(cond_ready, 1)
                    mf = mod[:].rearrange("p l m c -> p (l m) c")
                    with v.Fori(0, NS // 2) as i:
                        for s in range(2):
                            v.wait_ge(mod_mm, i * 2 + (s + 1))
                            v.tensor_copy(mf[:, i * 2 + s, :], ps[:, s, 0:2]).then_inc(mod_out, 1)
                    v.wait_ge(mod_out, NS)
                    for c in range(2):
                        link(v.tensor_tensor(mod[:, :, :, c], mod[:, :, :, c],
                                             vec[:, VEC["mod_b0"][0]:VEC["mod_b0"][0] + NS].rearrange("p (l m) -> p l m", l=2), ALU.add))
                    for c in range(2):
                        link(v.scalar_tensor_tensor(pre_s[:, :, :, c], mod[:, :, KT:2 * KT, c], 1.0,
                                                    vcol("norm_pre", 0, 2 * KT).rearrange("p (l k) -> p l k", l=2), ALU.add, ALU.mult))
                        link(v.tensor_tensor(post_s[:, :, :, c], mod[:, :, 2 * KT:3 * KT, c],
                                             vcol("norm_post", 0, 2 * KT).rearrange("p (l k) -> p l k", l=2), ALU.mult))

                @block.tensor
                def _(pe):
                    pe.wait_ge(cond_ready, 1)
                    with pe.Fori(0, NS // 4) as i:
                        for s in range(4):
                            pe.wait_ge(slab_in[s], i * 16 + 16)
                            pe.wait_ge(mod_out, i * 4 + (s - 1 if s >= 2 else 0))
                            for k in range(KT):
                                mm = pe.matmul(ps[:, s % 2, 0:2], wm[:, s, k, :], cond[:, k, :], start=k == 0, stop=k == KT - 1)
                            mm.then_inc(mod_mm, 1)

        def rms_stats(ph, tag, src, ntok, loads=None):
            blks = [(a, min(512, ntok - a)) for a in range(0, ntok, 512)]
            sq = ph.enter_context(nc.sbuf_tensor(f"sq_{tag}", [P, 2, ntok], F32))
            rstd = ph.enter_context(nc.sbuf_tensor(f"rstd_{tag}", [P, ntok], F32))
            s = {n: sem(f"{n}_{tag}") for n in ("sq_ready", "sq_used", "sum_ready", "root", "rstd_ready")}

            def scalar(act, ready):
                for k in range(KT):
                    ready(act, k)
                    if k >= 2:
                        act.wait_ge(s["sq_used"], k - 1)
                    act.activation(sq[:, k % 2, :], src(k), ACT.Square).then_inc(s["sq_ready"], 1)
                act.wait_ge(s["sum_ready"], 1)
                for b, (a, n) in enumerate(blks):
                    act.activation(rstd[:, a:a + n], ps[:, b, 0:n], ACT.Sqrt, scale=1.0 / D, bias=eps[:, 0:1]).then_inc(s["root"], 1)

            def tensor(pe):
                for k in range(KT):
                    pe.wait_ge(s["sq_ready"], k + 1)
                    for b, (a, n) in enumerate(blks):
                        mm = pe.matmul(ps[:, b, 0:n], ones[:], sq[:, k % 2, a:a + n], start=k == 0, stop=k == KT - 1)
                    mm.then_inc(s["sq_used"], 1)
                pe.matmul(ps[:, 7, 0:2], ones[:], ones[:, 0:2], start=True, stop=True).then_inc(s["sum_ready"], 1)

            def vector(v):
                v.wait_ge(s["root"], len(blks))
                v.reciprocal(rstd[:], rstd[:]).then_inc(s["rstd_ready"], 1)
                v.wait_ge(s["rstd_ready"], 1)

            return rstd, s["rstd_ready"], scalar, tensor, vector

        def pre_norm(v, act, layer, src, rstd, rstd_ready, xn, xn_ready, h, h_ready, spill=None):
            if v is not None:
                for k in range(KT):
                    if k >= 2:
                        v.wait_ge(h_ready, 2 * (k - 1))
                    v.tensor_tensor(xn[:, k % 2, :], src(k), rstd[:], ALU.mult).then_inc(xn_ready, 1)
            else:
                for k in range(KT):
                    act.wait_ge(xn_ready, k + 1)
                    for c, seg in ((1, slice(0, CTX)), (0, slice(CTX, T))):
                        act.activation(h[:, k, seg], xn[:, k % 2, seg], ACT.Identity,
                                       scale=pre_s[:, layer, k, c:c + 1], bias=mod[:, layer, k, c:c + 1]).then_inc(h_ready, 1)

        l0 = es.enter_context(ExitStack())
        xt = l0.enter_context(nc.sbuf_tensor("xt", [P, KT, T], F32))
        fgo = l0.enter_context(nc.sbuf_tensor("fgo", [P, KT, T], F32))
        h0 = l0.enter_context(nc.sbuf_tensor("h0", [P, KT, T], F32))
        with ExitStack() as ph:
            x_in = [sem(f"x_in{i}") for i in range(2)]
            xn = ph.enter_context(nc.sbuf_tensor("xn0", [P, 2, T], F32))
            xn_ready, h_ready = sem("xn0_ready"), sem("h0_ready")
            rstd, rr, f_act, f_pe, f_dve = rms_stats(ph, "pre0", lambda k: xt[:, k, :], T)
            with nc.Block() as block:
                @block.sync
                def _(sp):
                    for i in range(2):
                        ks = slice(i * KT // 2, (i + 1) * KT // 2)
                        sp.dma_start(xt[:, ks, :], A["xt"][ks].rearrange("k p t -> p k t")).then_inc(x_in[i], 16)

                @block.scalar
                def _(act):
                    f_act(act, lambda e, k: e.wait_ge(x_in[k // (KT // 2)], 16))
                    pre_norm(None, act, 0, None, None, None, xn, xn_ready, h0, h_ready)

                @block.tensor
                def _(pe):
                    f_pe(pe)

                @block.vector
                def _(v):
                    for i in range(2):
                        v.wait_ge(x_in[i], 16)
                    f_dve(v)
                    pre_norm(v, None, 0, lambda k: xt[:, k, :], rstd, rr, xn, xn_ready, h0, h_ready)

        with ExitStack() as ph:
            def sb(name, shape):
                return ph.enter_context(nc.sbuf_tensor(name, shape, F32))
            wi = sb("fw_slab", [P, 2, KT, P])
            ctab = sb("ctab", [P, 2, P])
            wmx = sb("wmix", [P, KT, P])
            cw = sb("cw", [P, KT, 2 * P])
            tl = sb("time_tab_lat", [P, KT, 2, HALF])
            alt = sb("alt", [P, 2])
            tc = sb("time_tab_ctx", [P, 2, 2, CTX])
            ub = sb("u_group", [P, T])
            zb = sb("z_group", [P, 1, T])
            ab = sb("ab_group", [P, NCH, 2 * P])
            qs = sb("q_part", [P, HALF])
            fb = sb("f_group", [P, T])
            tab_in, w_in_u, w_in_z = sem("tab_in"), sem("w_in_u"), sem("w_in_z")
            cwp, cwr = sem("cw_products"), sem("cw_ready")
            u_mm, z_mm, ab_mm, f_mm = sem("u_mm"), sem("z_mm"), sem("ab_mm"), sem("f_mm")
            u_out, zs_out, ab_out, q_out, f_out, fg_out, z_out = (sem("u_out"), sem("zs_out"), sem("ab_out"), sem("q_out"), sem("f_out"),
                                                                  sem("fg_out"), sem("z_out"))
            zsig = zb[:, 0, :]
            with nc.Block() as block:
                @block.sync
                def _(sp):
                    sp.dma_start(ctab[:], A["ctab"]).then_inc(tab_in, 16)
                    sp.dma_start(wmx[:], A["wmix"]).then_inc(tab_in, 16)
                    sp.dma_start(tl[:], A["tlat"]).then_inc(tab_in, 16)
                    sp.dma_start(alt[:], A["alt"]).then_inc(tab_in, 16)
                    sp.dma_start(tc[:], A["tctx"]).then_inc(tab_in, 16)
                    sp.dma_start(wi[:, 0], A["fwin"][0]).then_inc(w_in_u, 16)
                    sp.dma_start(wi[:, 1], A["fwin"][KT]).then_inc(w_in_z, 16)
                    with sp.Fori(1, KT) as g:
                        sp.wait_ge(u_mm, g * 3)
                        sp.dma_start(wi[:, 0], A["fwin"][g]).then_inc(w_in_u, 16)
                        sp.wait_ge(z_mm, g * 3)
                        sp.dma_start(wi[:, 1], A["fwin"][g + KT]).then_inc(w_in_z, 16)

                @block.tensor
                def _(pe):
                    pe.wait_ge(tab_in, 80)
                    for g in range(KT):
                        if g >= 4:
                            pe.wait_ge(cwr, g - 3)
                        for c in range(2):
                            mm = pe.matmul(ps[:, g % 4, c * P:c * P + P], ctab[:, c, :], wmx[:, g, :], start=True, stop=True)
                        mm.then_inc(cwp, 1)
                    pe.wait_ge(cwr, KT)
                    with pe.Fori(0, KT) as g:
                        for half, win, done, b0 in ((0, w_in_u, u_mm, 0), (1, w_in_z, z_mm, 3)):
                            pe.wait_ge(win, g * 16 + 16)
                            if half == 0:
                                pe.wait_ge(ab_out, g * 5)
                            else:
                                pe.wait_ge(f_out, g * 4)
                            for b, (a, n) in enumerate(BLK):
                                for k in range(KT):
                                    mm = pe.matmul(ps[:, b0 + b, 0:n], wi[:, half, k, :], h0[:, k, a:a + n], start=k == 0, stop=k == KT - 1)
                                mm.then_inc(done, 1)
                        pe.wait_ge(u_out, g * 3 + 3)
                        for q in range(NCH // 2):
                            for t in range(2):
                                mm = pe.matmul(ps[:, (6 + q) % 8, t * 256:t * 256 + 256], ub[:, (2 * q + t) * P:(2 * q + t + 1) * P],
                                               cw[:, g, :], start=True, stop=True)
                            mm.then_inc(ab_mm, 1)
                        pe.wait_ge(z_out, g * 3 + 3)
                        pe.wait_ge(ab_out, g * 5 + 5)
                        for c in range(2):
                            for t in range(KT):
                                mm = pe.matmul(ps[:, 3 + c, :], ab[:, 2 + t, c * P:c * P + P], tl[:, t, c, :], start=t == 0, stop=t == KT - 1)
                            mm.then_inc(f_mm, 1)
                        for t in range(KT):
                            mm = pe.matmul(ps[:, 5, CTX:CTX + 2], ab[:, 2 + t, 0:P], alt[:], start=t == 0, stop=t == KT - 1)
                        for c in range(2):
                            for t in range(2):
                                mm = pe.matmul(ps[:, 5, 0:CTX], ab[:, t, c * P:c * P + P], tc[:, t, c, :],
                                               start=c + t == 0, stop=c + t == 2)
                        mm.then_inc(f_mm, 1)

                @block.scalar
                def _(act):
                    for g in range(KT):
                        act.wait_ge(cwp, g + 1)
                        act.activation(cw[:, g, :], ps[:, g % 4, 0:2 * P], ACT.Copy).then_inc(cwr, 1)
                    act.wait_ge(cwr, KT)
                    with act.Fori(0, KT) as g:
                        for b, (a, n) in enumerate(BLK):
                            act.wait_ge(u_mm, g * 3 + (b + 1))
                            if b == 0:
                                act.wait_ge(ab_mm, g * 5)
                            act.activation(ub[:, a:a + n], ps[:, b, 0:n], ACT.Copy).then_inc(u_out, 1)
                        for b, (a, n) in enumerate(BLK):
                            act.wait_ge(z_mm, g * 3 + (b + 1))
                            if b == 0:
                                act.wait_ge(fg_out, g)
                            act.activation(zsig[:, a:a + n], ps[:, 3 + b, 0:n], ACT.Sigmoid).then_inc(zs_out, 1)
                        act.wait_ge(f_mm, g * 3 + 2)
                        act.activation(qs[:], ps[:, 4, :], ACT.Copy).then_inc(q_out, 1)

                @block.vector
                def _(v):
                    with v.Fori(0, KT) as g:
                        for b, (a, n) in enumerate(BLK):
                            v.wait_ge(zs_out, g * 3 + (b + 1))
                            v.tensor_tensor(zb[:, 0, a:a + n], zsig[:, a:a + n], ps[:, 3 + b, 0:n], ALU.mult).then_inc(z_out, 1)
                        for q in range(NCH // 2):
                            v.wait_ge(ab_mm, g * 5 + (q + 1))
                            v.tensor_copy(ab[:, 2 * q:2 * q + 2, :], ps[:, (6 + q) % 8, :].rearrange("p (t e) -> p t e", t=2)).then_inc(ab_out, 1)
                        v.wait_ge(f_mm, g * 3 + 3)
                        v.tensor_copy(fb[:, 0:CTX], ps[:, 5, 0:CTX]).then_inc(f_out, 1)
                        v.tensor_copy(fb[:, CTX + HALF:CTX + HALF + 1], ps[:, 5, CTX:CTX + 1]).then_inc(f_out, 1)
                        v.wait_ge(q_out, g + 1)
                        v.tensor_tensor(fb[:, CTX:CTX + HALF], ps[:, 3, :], qs[:], ALU.subtract).then_inc(f_out, 1)
                        v.tensor_tensor(fb[:, CTX + HALF + 1:T][:, ::-1], ps[:, 3, 1:HALF], qs[:, 1:HALF], ALU.add).then_inc(f_out, 1)
                        v.wait_ge(f_out, g * 4 + 4)
                        v.scalar_tensor_tensor(fgo[:, g, :], fb[:], vec[:, bass.ds(g + VEC["f_b_mix"][0], 1)], zb[:, 0, :],
                                               ALU.add, ALU.mult).then_inc(fg_out, 1)

        def out_proj(ph, tag, wts, src, dst, ntok):
            blks = [(a, min(512, ntok - a)) for a in range(0, ntok, 512)]
            nb = len(blks)
            w = ph.enter_context(nc.sbuf_tensor(f"wo_{tag}", [P, 2, KT, P], F32))
            w_in = [sem(f"wo_in{i}_{tag}") for i in range(2)]
            mm_done, out_done = sem(f"o_mm_{tag}"), sem(f"o_out_{tag}")
            with nc.Block() as block:
                @block.sync
                def _(sp):
                    for s in range(2):
                        sp.dma_start(w[:, s], wts[s]).then_inc(w_in[s], 16)
                    with sp.Fori(1, KT // 2) as i:
                        for s in range(2):
                            sp.wait_ge(mm_done, i * (2 * nb) + (s - 1) * nb)
                            sp.dma_start(w[:, s], wts[i * 2 + s]).then_inc(w_in[s], 16)

                @block.tensor
                def _(pe):
                    with pe.Fori(0, KT // 2) as i:
                        for s in range(2):
                            pe.wait_ge(w_in[s], i * 16 + 16)
                            for b, (a, n) in enumerate(blks):
                                if s == 1:
                                    pe.wait_ge(out_done, i * (2 * nb) + (b + 1))
                                else:
                                    pe.wait_ge(out_done, i * (2 * nb) )
                                for k in range(KT):
                                    mm = pe.matmul(ps[:, b, 0:n], w[:, s, k, :], src[:, k, a:a + n], start=k == 0, stop=k == KT - 1)
                                mm.then_inc(mm_done, 1)

                @block.scalar
                def _(act):
                    with act.Fori(0, KT // 2) as i:
                        for s in range(2):
                            for b, (a, n) in enumerate(blks):
                                act.wait_ge(mm_done, i * (2 * nb) + (s * nb + b + 1))
                                act.activation(dst[:, i * 2 + s, a:a + n], ps[:, b, 0:n], ACT.Copy).then_inc(out_done, 1)

        with ExitStack() as ph:
            out_proj(ph, "l0", A["fwout"], fgo, h0, T)

        with ExitStack() as ph:
            rstd, rr, f_act, f_pe, f_dve = rms_stats(ph, "post0", lambda k: h0[:, k, :], T)
            on = ph.enter_context(nc.sbuf_tensor("on0", [P, 2, T], F32))
            on_ready, x_ready, on_chain = sem("on0_ready"), sem("x1_ready"), sem("on0_chain")
            with nc.Block() as block:
                @block.scalar
                def _(act):
                    f_act(act, lambda e, k: None)

                @block.tensor
                def _(pe):
                    f_pe(pe)

                @block.vector
                def _(v):
                    f_dve(v)
                    for k in range(KT):
                        if k >= 2:
                            v.wait_ge(x_ready, 2 * (k - 1))
                        v.tensor_tensor(on[:, k % 2, :], h0[:, k, :], rstd[:], ALU.mult).then_inc(on_ready, 1)
                        v.wait_ge(on_ready, k + 1)
                        for c, seg in ((1, slice(0, CTX)), (0, slice(CTX, T))):
                            v.scalar_tensor_tensor(xt[:, k, seg], on[:, k % 2, seg], post_s[:, 0, k, c:c + 1], xt[:, k, seg],
                                                   ALU.mult, ALU.add).then_inc(x_ready, 1)
        with ExitStack() as ph:
            xn = ph.enter_context(nc.sbuf_tensor("xn1", [P, 2, T], F32))
            xn_ready, h_ready, spill = sem("xn1_ready"), sem("h1_ready"), sem("x1_spilled")
            rstd, rr, f_act, f_pe, f_dve = rms_stats(ph, "pre1", lambda k: xt[:, k, :], T)
            with nc.Block() as block:
                @block.sync
                def _(sp):
                    sp.dma_start(x1_d, xt[:, :, CTX:T]).then_inc(spill, 16)
                    sp.wait_ge(spill, 16)

                @block.scalar
                def _(act):
                    f_act(act, lambda e, k: None)
                    pre_norm(None, act, 1, None, None, None, xn, xn_ready, h0, h_ready)

                @block.tensor
                def _(pe):
                    f_pe(pe)

                @block.vector
                def _(v):
                    f_dve(v)
                    pre_norm(v, None, 1, lambda k: xt[:, k, :], rstd, rr, xn, xn_ready, h0, h_ready)

        GW = 64
        with ExitStack() as ph:
            nb_ = ph.enter_context(nc.sbuf_tensor("neighbours", [P, 2, T], F32))
            sc_, sd = sem("shift_chain"), sem("shift_done")
            pc_ = sem("shift_pool")
            with nc.Block() as block:
                @block.vector
                def _(v):
                    n = [0]

                    def link(ins):
                        n[0] += 1
                        ins.then_inc(sc_, 1)
                        v.wait_ge(sc_, n[0])

                    for k in range(KT):
                        s = nb_[:, k % 2, :]
                        h = h0[:, k, :]
                        sl, hl = s[:, CTX:T], h[:, CTX:T]
                        sg = sl.rearrange("p (r w) -> p r w", w=GW)
                        hg = hl.rearrange("p (r w) -> p r w", w=GW)
                        link(v.tensor_tensor(sl[:, GW:LAT - GW], hl[:, 0:LAT - 2 * GW], hl[:, 2 * GW:LAT], ALU.add))
                        link(v.tensor_copy(sl[:, 0:GW], hl[:, GW:2 * GW]))
                        link(v.tensor_copy(sl[:, LAT - GW:LAT], hl[:, LAT - 2 * GW:LAT - GW]))
                        link(v.tensor_tensor(sg[:, :, 1:GW], sg[:, :, 1:GW], hg[:, :, 0:GW - 1], ALU.add))
                        link(v.tensor_tensor(sg[:, :, 0:GW - 1], sg[:, :, 0:GW - 1], hg[:, :, 1:GW], ALU.add))
                        link(v.scalar_tensor_tensor(fgo[:, k, CTX:T], sl, 0.25, hl, ALU.mult, ALU.subtract))
                        link(v.tensor_tensor(s[:, 1:CTX - 1], h[:, 0:CTX - 2], h[:, 2:CTX], ALU.add))
                        link(v.tensor_copy(s[:, 0:1], h[:, 1:2]))
                        link(v.tensor_copy(s[:, CTX - 1:CTX], h[:, CTX - 2:CTX - 1]))
                        link(v.scalar_tensor_tensor(fgo[:, k, 0:CTX], s[:, 0:CTX], 0.5, h[:, 0:CTX], ALU.mult, ALU.subtract))

        dl, h1 = fgo, h0

        def mix(ph, tag, m, lo):
            done = sem(f"mixed_{tag}")

            def vector(v):
                for k in range(KT):
                    v.scalar_tensor_tensor(xt[:, k, lo:T], dl[:, k, lo:T], vcol("mu", m * KT + k), h1[:, k, lo:T],
                                           ALU.mult, ALU.add).then_inc(done, 1)
            return done, vector

        def project(pe, w_in, w_at, done, free, src, blks, i):
            nb = len(blks)
            pe.wait_ge(w_in, i * 16 + 16)
            for b, (a, n) in enumerate(blks):
                pe.wait_ge(free, i * nb)
                for k in range(KT):
                    mm = pe.matmul(ps[:, b, 0:n], w_at[:, k, :], src[:, k, a:a + n], start=k == 0, stop=k == KT - 1)
                mm.then_inc(done, 1)

        lo_ = es.enter_context(ExitStack())
        hid = lo_.enter_context(nc.sbuf_tensor("lora_hidden", [P, 2, T], F32))
        for m, (mu_i, name) in enumerate(((4, "w"), (5, "a"))):
            with ExitStack() as ph:
                mixed, f_mix = mix(ph, f"lora_{name}", mu_i, 0)
                w1 = ph.enter_context(nc.sbuf_tensor(f"lora_{name}1", [P, KT, P], F32))
                w_in, mm_done, out_done = sem(f"l1_in_{name}"), sem(f"l1_mm_{name}"), sem(f"l1_out_{name}")
                with nc.Block() as block:
                    @block.sync
                    def _(sp):
                        sp.dma_start(w1[:], A["w1" if m == 0 else "a1"]).then_inc(w_in, 16)

                    @block.vector
                    def _(v):
                        f_mix(v)

                    @block.tensor
                    def _(pe):
                        pe.wait_ge(w_in, 16)
                        for k in range(KT):
                            pe.wait_ge(mixed, k + 1)
                            for b, (a, n) in enumerate(BLK):
                                mm = pe.matmul(ps[:, b, 0:n], w1[:, k, :], xt[:, k, a:a + n], start=k == 0, stop=k == KT - 1)
                        mm.then_inc(mm_done, 1)

                    @block.scalar
                    def _(act):
                        act.wait_ge(mm_done, 1)
                        for b, (a, n) in enumerate(BLK):
                            act.activation(hid[:, m, a:a + n], ps[:, b, 0:n], ACT.Tanh if m == 0 else ACT.Copy).then_inc(out_done, 1)

        with ExitStack() as ph:
            w2 = ph.enter_context(nc.sbuf_tensor("lora_up", [P, 2, P], F32))
            sw = ph.enter_context(nc.sbuf_tensor("sw_out", [P, NDIR, T], F32))
            sa = ph.enter_context(nc.sbuf_tensor("sa_out", [P, NDIR, T], F32))
            w_in, up_mm, up_out, sw_st, sa_st = sem("l2_in"), sem("l2_mm"), sem("l2_out"), sem("sw_stored"), sem("sa_stored")
            with nc.Block() as block:
                @block.sync
                def _(sp):
                    with sp.Fori(0, KT) as j:
                        sp.wait_ge(up_mm, j * 4)
                        sp.dma_start(w2[:], A["w2a2"][j]).then_inc(w_in, 16)
                        sp.wait_ge(up_out, j * 12 + 6)
                        for d in range(NDIR):
                            sp.dma_start(fe_v[j, :, FEATS.index("sw"), d], sw[:, d].rearrange("p (c t) -> p c t", t=CH)).then_inc(sw_st, 16)
                        sp.wait_ge(up_out, j * 12 + 12)
                        sp.dma_start(sa_d[j], sa[:]).then_inc(sa_st, 16)
                    sp.wait_ge(sw_st, KT * 32)
                    sp.wait_ge(sa_st, KT * 16)

                @block.tensor
                def _(pe):
                    with pe.Fori(0, KT) as j:
                        pe.wait_ge(w_in, j * 16 + 16)
                        for q in range(4):
                            m, d = q // 2, q % 2
                            b0 = 3 * d
                            if m == 0:
                                pe.wait_ge(up_out, j * 12)
                            else:
                                pe.wait_ge(up_out, j * 12 + 3 * (d + 1))
                            for b, (a, n) in enumerate(BLK):
                                mm = pe.matmul(ps[:, b0 + b, 0:n], w2[d * LORA:(d + 1) * LORA, m, :],
                                               hid[d * LORA:(d + 1) * LORA, m, a:a + n], start=True, stop=True)
                            mm.then_inc(up_mm, 1)

                @block.scalar
                def _(act):
                    with act.Fori(0, KT) as j:
                        for q in range(4):
                            m, d = q // 2, q % 2
                            act.wait_ge(up_mm, j * 4 + (q + 1))
                            if q == 0:
                                act.wait_ge(sw_st, j * 32)
                            if q == 2:
                                act.wait_ge(sa_st, j * 16)
                            dst = (sw, sa)[m]
                            for b, (a, n) in enumerate(BLK):
                                if m == 0 and d == 1:
                                    pieces = [(x, y) for x, y in ((max(a, 0), min(a + n, CTX)), (max(a, CTX), min(a + n, T))) if y > x]
                                else:
                                    pieces = [(a, a + n)]
                                for x, y in pieces:
                                    if m == 0 and d == 1:
                                        lo, hi = (CTX - y, CTX - x) if y <= CTX else (CTX + T - y, CTX + T - x)
                                        out = dst[:, d, lo:hi][:, ::-1]
                                    else:
                                        out = dst[:, d, x:y]
                                    ins = act.activation(out, ps[:, 3 * d + b, x - a:y - a], ACT.Sigmoid,
                                                         bias=vec[:, bass.ds(j + (VEC[("w0", "a0")[m]][0] + d * KT), 1)])
                                ins.then_inc(up_out, 1)
        lo_.close()

        def rev_copy(v, dst, src):
            a = v.tensor_copy(dst[:, 0:CTX][:, ::-1], src[:, 0:CTX])
            b = v.tensor_copy(dst[:, CTX:T][:, ::-1], src[:, CTX:T])
            return a, b

        with ExitStack() as ph:
            def sb(name, shape):
                return ph.enter_context(nc.sbuf_tensor(name, shape, F32))
            mixed, f_mix = mix(ph, "k", 1, 0)
            w = sb("wk_slab", [P, KT, P])
            kn, kk0, kk, sq, inv, ksum = (sb(n, [P, T]) for n in ("k_nat", "kk_raw", "kk_nat", "kk_sq", "kk_inv", "k_sum"))
            sa, am = sb("iclr", [P, NDIR, T]), sb("k_factor", [P, NDIR, T])
            fo = sb("k_feats", [P, 3, T])
            w_in, sa_in, k_mm, k_out, sq_rdy, n_mm, root, chain, kd_st, pch = (
                sem("wk_in"), sem("iclr_in"), sem("k_mm"), sem("k_out"), sem("kk_sq_ready"), sem("kk_norm_mm"), sem("kk_root"),
                sem("k_chain"), sem("k_stored"), sem("k_pool"))
            NL = 17
            fo_ready = sem("k_feats_ready")
            with nc.Block() as block:
                @block.sync
                def _(sp):
                    with sp.Fori(0, KT) as j:
                        sp.wait_ge(k_mm, j * 3)
                        sp.dma_start(w[:], A["rwin"][j + KT]).then_inc(w_in, 16)
                        sp.wait_ge(chain, j * NL)
                        sp.dma_start(sa[:], sa_d[j]).then_inc(sa_in, 16)
                        for d in range(NDIR):
                            sp.wait_ge(fo_ready, j * 2 + (d + 1))
                            for f in range(3):
                                sp.dma_start(fe_v[j, :, f, d], fo[:, f].rearrange("p (c t) -> p c t", t=CH)).then_inc(kd_st, 16)
                            if d == 1:
                                sp.dma_start(ks_d[j], ksum[:, CTX:T]).then_inc(kd_st, 16)
                    sp.wait_ge(kd_st, KT * 7 * 16)

                @block.tensor
                def _(pe):
                    for k in range(KT):
                        pe.wait_ge(mixed, k + 1)
                    with pe.Fori(0, KT) as j:
                        project(pe, w_in, w, k_mm, k_out, xt, BLK, j)
                        pe.wait_ge(sq_rdy, j + 1)
                        pe.wait_ge(root, j * 3)
                        for b, (a, n) in enumerate(BLK):
                            mm = pe.matmul(ps[:, 3 + b, 0:n], hones[:], sq[:, a:a + n], start=True, stop=True)
                        mm.then_inc(n_mm, 1)

                @block.scalar
                def _(act):
                    with act.Fori(0, KT) as j:
                        for b, (a, n) in enumerate(BLK):
                            act.wait_ge(k_mm, j * 3 + (b + 1))
                            if b == 0:
                                act.wait_ge(chain, j * NL)
                            act.activation(kn[:, a:a + n], ps[:, b, 0:n], ACT.Copy).then_inc(k_out, 1)
                        act.wait_ge(n_mm, j + 1)
                        for b, (a, n) in enumerate(BLK):
                            act.activation(inv[:, a:a + n], ps[:, 3 + b, 0:n], ACT.Sqrt).then_inc(root, 1)

                @block.gpsimd
                def _(g):
                    with g.Fori(0, KT) as j:
                        g.wait_ge(chain, j * NL + 1)
                        g.tensor_tensor(sq[:], kk0[:], kk0[:], ALU.mult).then_inc(sq_rdy, 1)

                @block.vector
                def _(v):
                    f_mix(v)
                    with v.Fori(0, KT) as j:
                        n = [0]

                        def link(ins, wait=True):
                            n[0] += 1
                            ins.then_inc(chain, 1)
                            if wait:
                                v.wait_ge(chain, j * NL + n[0])

                        kv = lambda name: vec[:, bass.ds(j + VEC[name][0], 1)]
                        v.wait_ge(k_out, j * 3 + 3)
                        link(v.tensor_scalar(kk0[:], kn[:], kv("k_k"), None, ALU.mult))
                        v.wait_ge(sa_in, j * 16 + 16)
                        for d in range(NDIR):
                            link(v.tensor_scalar(am[:, d], sa[:, d], kv("k_a"), kam[:, bass.ds(j, 1)], ALU.mult, ALU.add))
                        v.wait_ge(kd_st, j * 7 * 16)
                        link(v.tensor_tensor(ksum[:], am[:, 0], am[:, 1], ALU.add))
                        link(v.tensor_tensor(ksum[:], ksum[:], kn[:], ALU.mult))
                        v.wait_ge(root, j * 3 + 3)
                        link(v.tensor_scalar(inv[:], inv[:], 1e-12, None, ALU.max))
                        link(v.reciprocal(inv[:], inv[:]))
                        link(v.tensor_tensor(kk[:], kk0[:], inv[:], ALU.mult))
                        link(v.tensor_tensor(fo[:, 0], kn[:], am[:, 0], ALU.mult), False)
                        link(v.tensor_tensor(fo[:, 1], kk[:], sa[:, 0], ALU.mult), False)
                        link(v.tensor_scalar(fo[:, 2], kk[:], -1.0, None, ALU.mult))
                        v.tensor_copy(am[:, 0, 0:1], am[:, 0, 0:1]).then_inc(fo_ready, 1)
                        v.wait_ge(kd_st, j * 7 * 16 + 48)
                        for lo, hi in ((0, CTX), (CTX, T)):
                            r = slice(lo, hi)
                            link(v.tensor_tensor(fo[:, 0, r][:, ::-1], kn[:, r], am[:, 1, r], ALU.mult), False)
                            link(v.tensor_tensor(fo[:, 1, r][:, ::-1], kk[:, r], sa[:, 1, r], ALU.mult), False)
                            link(v.tensor_scalar(fo[:, 2, r][:, ::-1], kk[:, r], -1.0, None, ALU.mult), lo > 0)
                        v.tensor_copy(am[:, 1, 0:1], am[:, 1, 0:1]).then_inc(fo_ready, 1)
                        assert n[0] == NL, n

        with ExitStack() as ph:
            def sb(name, shape):
                return ph.enter_context(nc.sbuf_tensor(name, shape, F32))
            mixed, f_mix = mix(ph, "v", 2, 0)
            w = sb("wv_slab", [P, KT, P])
            vo = sb("v_out", [P, NDIR, T])
            w_in, v_mm, v_out, v_rev, v_st = sem("wv_in"), sem("v_mm"), sem("v_out"), sem("v_reversed"), sem("v_stored")
            with nc.Block() as block:
                @block.sync
                def _(sp):
                    with sp.Fori(0, KT) as j:
                        sp.wait_ge(v_mm, j * 3)
                        sp.dma_start(w[:], A["rwin"][j + 2 * KT]).then_inc(w_in, 16)
                        sp.wait_ge(v_out, j * 3 + 3)
                        sp.wait_ge(v_rev, j * 2 + 2)
                        for d in range(NDIR):
                            sp.dma_start(fe_v[j, :, FEATS.index("v"), d], vo[:, d].rearrange("p (c t) -> p c t", t=CH)).then_inc(v_st, 16)
                    sp.wait_ge(v_st, KT * 32)

                @block.tensor
                def _(pe):
                    for k in range(KT):
                        pe.wait_ge(mixed, k + 1)
                    with pe.Fori(0, KT) as j:
                        project(pe, w_in, w, v_mm, v_out, xt, BLK, j)

                @block.scalar
                def _(act):
                    with act.Fori(0, KT) as j:
                        for b, (a, n) in enumerate(BLK):
                            act.wait_ge(v_mm, j * 3 + (b + 1))
                            if b == 0:
                                act.wait_ge(v_st, j * 32)
                            act.activation(vo[:, 0, a:a + n], ps[:, b, 0:n], ACT.Copy).then_inc(v_out, 1)

                @block.vector
                def _(v):
                    f_mix(v)
                    with v.Fori(0, KT) as j:
                        v.wait_ge(v_out, j * 3 + 3)
                        for ins in rev_copy(v, vo[:, 1], vo[:, 0]):
                            ins.then_inc(v_rev, 1)

        LB = [(CTX, 512), (CTX + 512, 512)]
        with ExitStack() as ph:
            def sb(name, shape):
                return ph.enter_context(nc.sbuf_tensor(name, shape, F32))
            mixed, f_mix = mix(ph, "r", 0, CTX)
            w = sb("wr_slab", [P, KT, P])
            ro = sb("r_out", [P, NDIR, T])
            ks, vn, rk, bv = (sb(n, [P, LAT]) for n in ("ks_in", "v_in", "rk", "bonus"))
            w_in, kv_in, r_mm, r_out, r_rev, r_st, rkc, b_mm, b_out, b_st, zr = (
                sem("wr_in"), sem("kv_in"), sem("r_mm"), sem("r_out"), sem("r_reversed"), sem("r_stored"), sem("rk_chain"),
                sem("b_mm"), sem("b_out"), sem("b_stored"), sem("r_zero"))
            with nc.Block() as block:
                @block.sync
                def _(sp):
                    with sp.Fori(0, KT) as j:
                        sp.wait_ge(r_mm, j * 2)
                        sp.dma_start(w[:], A["rwin"][j]).then_inc(w_in, 16)
                        sp.wait_ge(b_out, j)
                        sp.dma_start(ks[:], ks_d[j]).then_inc(kv_in, 16)
                        sp.dma_start(vn[:].rearrange("p (c t) -> p c t", t=CH), fe_v[j, :, FEATS.index("v"), 0, 2:NCH]).then_inc(kv_in, 16)
                        sp.wait_ge(r_out, j * 2 + 2)
                        sp.wait_ge(r_rev, j * 2 + 2)
                        for d in range(NDIR):
                            sp.dma_start(fe_v[j, :, FEATS.index("r"), d], ro[:, d].rearrange("p (c t) -> p c t", t=CH)).then_inc(r_st, 16)
                        sp.wait_ge(b_out, j + 1)
                        sp.dma_start(bv_d[j], bv[:]).then_inc(b_st, 16)
                    sp.wait_ge(r_st, KT * 32)
                    sp.wait_ge(b_st, KT * 16)

                @block.tensor
                def _(pe):
                    for k in range(KT):
                        pe.wait_ge(mixed, k + 1)
                    with pe.Fori(0, KT) as j:
                        project(pe, w_in, w, r_mm, r_out, xt, LB, j)
                        pe.wait_ge(rkc, j * 2 + 2)
                        pe.wait_ge(b_out, j)
                        for b in range(2):
                            mm = pe.matmul(ps[:, 3 + b, :], hones[:], rk[:, b * 512:(b + 1) * 512], start=True, stop=True)
                        mm.then_inc(b_mm, 1)

                @block.scalar
                def _(act):
                    with act.Fori(0, KT) as j:
                        for b, (a, n) in enumerate(LB):
                            act.wait_ge(r_mm, j * 2 + (b + 1))
                            if b == 0:
                                act.wait_ge(r_st, j * 32)
                                act.wait_ge(rkc, j * 2)
                            act.activation(ro[:, 0, a:a + n], ps[:, b, 0:n], ACT.Copy).then_inc(r_out, 1)

                @block.vector
                def _(v):
                    f_mix(v)
                    v.memset(ro[:, :, 0:CTX], 0.0).then_inc(zr, 1)
                    v.wait_ge(zr, 1)
                    with v.Fori(0, KT) as j:
                        v.wait_ge(r_out, j * 2 + 2)
                        for a in (0, HALF):
                            v.tensor_copy(ro[:, 1, T - a - HALF:T - a][:, ::-1], ro[:, 0, CTX + a:CTX + a + HALF]).then_inc(r_rev, 1)
                        v.wait_ge(kv_in, j * 32 + 32)
                        v.tensor_tensor(rk[:], ro[:, 0, CTX:T], ks[:], ALU.mult).then_inc(rkc, 1)
                        v.wait_ge(rkc, j * 2 + 1)
                        v.tensor_scalar(rk[:], rk[:], vec[:, bass.ds(j + VEC["r_k"][0], 1)], None, ALU.mult).then_inc(rkc, 1)
                        v.wait_ge(b_mm, j + 1)
                        v.wait_ge(b_st, j * 16)
                        v.tensor_tensor(bv[:].rearrange("p (b t) -> p b t", b=2), ps[:, 3:5, :], vn[:].rearrange("p (b t) -> p b t", b=2),
                                        ALU.mult).then_inc(b_out, 1)

        with ExitStack() as ph:
            def sb(name, shape):
                return ph.enter_context(nc.sbuf_tensor(name, shape, F32))
            mixed, f_mix = mix(ph, "g", 3, CTX)
            w = sb("wg_slab", [P, KT, P])
            go, gs = sb("g_out", [P, LAT]), sb("g_sig", [P, LAT])
            w_in, g_mm, g_sig, g_out, g_st = sem("wg_in"), sem("g_mm"), sem("g_sig"), sem("g_out"), sem("g_stored")
            with nc.Block() as block:
                @block.sync
                def _(sp):
                    with sp.Fori(0, KT) as j:
                        sp.wait_ge(g_mm, j * 2)
                        sp.dma_start(w[:], A["rwin"][j + 3 * KT]).then_inc(w_in, 16)
                        sp.wait_ge(g_out, j * 2 + 2)
                        sp.dma_start(gz_d[j], go[:]).then_inc(g_st, 16)
                    sp.wait_ge(g_st, KT * 16)

                @block.tensor
                def _(pe):
                    for k in range(KT):
                        pe.wait_ge(mixed, k + 1)
                    with pe.Fori(0, KT) as j:
                        project(pe, w_in, w, g_mm, g_out, xt, LB, j)

                @block.scalar
                def _(act):
                    with act.Fori(0, KT) as j:
                        for b in range(2):
                            act.wait_ge(g_mm, j * 2 + (b + 1))
                            act.wait_ge(g_out, j * 2)
                            act.activation(gs[:, b * 512:(b + 1) * 512], ps[:, b, :], ACT.Sigmoid).then_inc(g_sig, 1)

                @block.vector
                def _(v):
                    f_mix(v)
                    with v.Fori(0, KT) as j:
                        for b in range(2):
                            v.wait_ge(g_sig, j * 2 + (b + 1))
                            v.wait_ge(g_st, j * 16)
                            v.tensor_tensor(go[:, b * 512:(b + 1) * 512], gs[:, b * 512:(b + 1) * 512], ps[:, b, :], ALU.mult).then_inc(g_out, 1)

        l0.close()
        scan(nc, es, sem, ps, ident, eps, fe_d, y_d)

        fin = es.enter_context(ExitStack())
        gl = fin.enter_context(nc.sbuf_tensor("gated", [P, KT, LAT], F32))
        with ExitStack() as ph:
            def sb(name, shape):
                return ph.enter_context(nc.sbuf_tensor(name, shape, F32))
            yi, bi, gi = sb("y_in", [P, NDIR, LAT]), sb("bonus_in", [P, LAT]), sb("gate_in", [P, LAT])
            y, yc, sq, sd_ = (sb(n, [P, LAT]) for n in ("y", "y_centred", "y_sq", "y_std"))
            y_in, bg_in, chain, m_mm, sqr, v_mm, root = (sem("y_in"), sem("bg_in"), sem("y_chain"), sem("mean_mm"), sem("y_sq_ready"),
                                                        sem("var_mm"), sem("y_root"))
            NL = 9
            b2 = lambda t: t[:].rearrange("p (b t) -> p b t", b=2)
            with nc.Block() as block:
                @block.sync
                def _(sp):
                    with sp.Fori(0, KT) as j:
                        sp.wait_ge(chain, j * NL)
                        for d in range(NDIR):
                            sp.dma_start(yi[:, d].rearrange("p (c t) -> p c t", t=CH), y_v[j, :, d, 2:NCH]).then_inc(y_in, 16)
                        sp.dma_start(bi[:], bv_d[j]).then_inc(bg_in, 16)
                        sp.dma_start(gi[:], gz_d[j]).then_inc(bg_in, 16)

                @block.tensor
                def _(pe):
                    with pe.Fori(0, KT) as j:
                        pe.wait_ge(chain, j * NL + 1)
                        for b in range(2):
                            mm = pe.matmul(ps[:, b, :], hones[:], y[:, b * 512:(b + 1) * 512], start=True, stop=True)
                        mm.then_inc(m_mm, 1)
                        pe.wait_ge(sqr, j + 1)
                        for b in range(2):
                            mm = pe.matmul(ps[:, 2 + b, :], hones[:], sq[:, b * 512:(b + 1) * 512], start=True, stop=True)
                        mm.then_inc(v_mm, 1)

                @block.scalar
                def _(act):
                    with act.Fori(0, KT) as j:
                        act.wait_ge(chain, j * NL + 2)
                        act.activation(sq[:], yc[:], ACT.Square).then_inc(sqr, 1)
                        act.wait_ge(v_mm, j + 1)
                        act.activation(b2(sd_), ps[:, 2:4, :], ACT.Sqrt, scale=1.0 / HD, bias=eps[:, 1:2]).then_inc(root, 1)

                @block.vector
                def _(v):
                    with v.Fori(0, KT) as j:
                        n = [0]

                        def link(ins):
                            n[0] += 1
                            ins.then_inc(chain, 1)
                            v.wait_ge(chain, j * NL + n[0])

                        kv = lambda name: vec[:, bass.ds(j + VEC[name][0], 1)]
                        v.wait_ge(y_in, j * 32 + 32)
                        link(v.tensor_tensor(y[:], yi[:, 0], yi[:, 1][:, ::-1], ALU.add))
                        v.wait_ge(m_mm, j + 1)
                        link(v.scalar_tensor_tensor(b2(yc), ps[:, 0:2, :], -1.0 / HD, b2(y), ALU.mult, ALU.add))
                        v.wait_ge(root, j + 1)
                        link(v.reciprocal(sd_[:], sd_[:]))
                        link(v.tensor_tensor(yc[:], yc[:], sd_[:], ALU.mult))
                        link(v.tensor_scalar(yc[:], yc[:], kv("ln_w"), kv("ln_b"), ALU.mult, ALU.add))
                        v.wait_ge(bg_in, j * 32 + 32)
                        link(v.tensor_tensor(yc[:], yc[:], bi[:], ALU.add))
                        link(v.tensor_tensor(gl[:, j, :], yc[:], gi[:], ALU.mult))
                        link(v.tensor_copy(y[:, 0:1], y[:, 0:1]))
                        link(v.tensor_copy(y[:, 0:1], y[:, 0:1]))
                        assert n[0] == NL

        ol = fin.enter_context(nc.sbuf_tensor("o_last", [P, KT, LAT], F32))
        with ExitStack() as ph:
            out_proj(ph, "l1", A["rwout"], gl, ol, LAT)
        with ExitStack() as ph:
            rstd, rr, f_act, f_pe, f_dve = rms_stats(ph, "post1", lambda k: ol[:, k, :], LAT)
            x1 = ph.enter_context(nc.sbuf_tensor("x1", [P, KT, LAT], F32))
            x_in, on_ready, o_ready, st = sem("x1_in"), sem("on1_ready"), sem("out_ready"), sem("out_stored")
            with nc.Block() as block:
                @block.sync
                def _(sp):
                    sp.dma_start(x1[:], x1_d).then_inc(x_in, 16)
                    for k in range(KT):
                        sp.wait_ge(o_ready, k + 1)
                        sp.dma_start(A["out"][k], x1[:, k, :]).then_inc(st, 16)
                    sp.wait_ge(st, KT * 16)

                @block.scalar
                def _(act):
                    f_act(act, lambda e, k: None)

                @block.tensor
                def _(pe):
                    f_pe(pe)

                @block.vector
                def _(v):
                    f_dve(v)
                    v.wait_ge(x_in, 16)
                    for k in range(KT):
                        v.tensor_tensor(ol[:, k, :], ol[:, k, :], rstd[:], ALU.mult).then_inc(on_ready, 1)
                        v.wait_ge(on_ready, k + 1)
                        v.scalar_tensor_tensor(x1[:, k, :], ol[:, k, :], post_s[:, 1, k, 0:1], x1[:, k, :],
                                               ALU.mult, ALU.add).then_inc(o_ready, 1)


LEVELS = (2, 4, 8, 16, 32, 64)
STEPS = ["at", "a", "akt", "tok1", "tok2", "rbt", "rkt", "t2", "lv"]
for _k in LEVELS:
    STEPS += ([f"t{_k}"] if _k > 2 else []) + ([f"m{_k}"] if _k < 64 else []) + [f"mt{_k}"]
STEPS += ["wt", "sa", "y", "st"]
NSTEP = len(STEPS)
EMPTIED = {n: "D" for n in STEPS}
EMPTIED.update({n: "A" for n in ["at", "tok1", "tok2", "lv", "sa", "y", "mt64"] + [f"m{k}" for k in LEVELS if k < 64]})
A_ORDER = [n for n in STEPS if EMPTIED[n] == "A"]
D_ORDER = [n for n in STEPS if EMPTIED[n] == "D"]
D_ORDER.insert(D_ORDER.index("a") + 1, "mt2_init")
D_ORDER.insert(D_ORDER.index("wt"), "wt_head0")
D_ORDER.insert(D_ORDER.index("st"), "st_head0")
D_ORDER += ["st_scaled_head0", "st_scaled"]


def scan(nc, es, sem, ps, ident, eps, fe_d, y_d):
    NIT = KT * NCC
    U = 4
    ph = es.enter_context(ExitStack())

    def sb(name, shape, dt=F32):
        return ph.enter_context(nc.sbuf_tensor(name, shape, dt))

    two = range(2)
    feat = [sb(f"feat{s}", [P, NF, NDIR, CH]) for s in two]
    cum = [sb(f"cum{s}", [P, NDIR, CH]) for s in two]
    cumx = [sb(f"cumx{s}", [P, NDIR, CH]) for s in two]
    ex = [sb(f"exps{s}", [P, 3, NDIR, CH]) for s in two]
    pc, pcu = [sb(f"pend{s}", [P, NDIR]) for s in two], [sb(f"pend_used{s}", [P, NDIR]) for s in two]
    at, bt, kt, rt = ([sb(f"{n}{s}", [P, NDIR, CH]) for s in two] for n in ("at", "bt", "kt", "rt"))
    atz, btz, ktz, WTz = ([sb(f"{n}{s}", [P, 2, NDIR, CH]) for s in two] for n in ("atz", "btz", "ktz", "WTz"))
    big = lambda n: [sb(f"{n}{s}", [P, U, CH]) for s in two]
    AT, AKT, RBT, RKT, M2, MT2, M, MT, TOK1, TOK2 = (big(n) for n in ("AT", "AKT", "RBT", "RKT", "M2", "MT2", "M", "MT", "TOK1_", "TOK2_"))
    TT = {k: big(f"TT{k}_") for k in LEVELS}
    LV, SA = ([sb(f"{n}{s}", [P, U, HD]) for s in two] for n in ("LV", "SA"))
    Y = [sb(f"Y{s}", [P, NDIR, CH]) for s in two]
    Sz, stmp = sb("Sz", [P, 2, NDIR, HD]), sb("S_sum", [P, NDIR, HD])
    hmask = sb("head_mask", [P, 2])
    keep = sb("keep", [P, NIT + NCC])
    restart = sb("restart", [P, NDIR * CH])
    ml = {k: sb(f"mask{k}", [P, CH], I32) for k in (1,) + LEVELS}
    mt1 = sb("mask1t", [P, CH], I32)
    tick = sb("tick", [P, 2 * len(D_ORDER)])
    mstrict, mincl = sb("mask_strict", [P, CH], I32), sb("mask_incl", [P, CH], I32)

    ld, cumr, cumxr, expr, xp, rtr, pes, evA, evD, yst = ([sem(f"{n}{s}") for s in two] for n in (
        "feat_in", "cum_ready", "cumx_ready", "exp_ready", "operands_ready", "rt_ready", "step_done", "act_emptied", "dve_emptied", "y_stored"))
    init, msk = sem("scan_init"), sem("mask_ready")
    NA, ND = len(A_ORDER), len(D_ORDER)
    NXP = 9

    def emptied(eng, s, it, name):
        if name in D_ORDER:
            eng.wait_ge(evD[s], it * ND + (D_ORDER.index(name) + 1))
        else:
            eng.wait_ge(evA[s], it * NA + (A_ORDER.index(name) + 1))

    def done(eng, s, it, name):
        eng.wait_ge(pes[s], it * NSTEP + (STEPS.index(name) + 1))

    def bank(s, name):
        return 4 * s + STEPS.index(name) % 4

    def psv(s, name, n=CH):
        return ps[:, bank(s, name), 0:U * n].rearrange("p (u t) -> p u t", u=U)

    bc = lambda m: m[:].unsqueeze(1).broadcast_to([P, U, CH])
    units = [(d, h) for d in range(NDIR) for h in range(2)]
    hp = lambda h: slice(h * HD, (h + 1) * HD)

    with nc.Block() as block:
        @block.gpsimd
        def _(g):
            n = [0]

            def link(ins):
                n[0] += 1
                ins.then_inc(msk, 1)
                g.wait_ge(msk, n[0])

            for k in (1,) + LEVELS:
                m = ml[k]
                link(g.memset(m[:], 1))
                v4 = m[:].rearrange("p (b e c) -> p b e c", e=2, c=k)
                link(g.memset(v4[:, :, 1, :], 0))
                v3 = m[:].rearrange("p (b q) -> p b q", q=2 * k)
                link(g.affine_select(out=v3, in_=v3, compare_op=ALU.is_ge, fill=0, base=-k, pattern=[[-2 * k, CH // (2 * k)], [0, 2 * k]], channel_multiplier=1))
                link(g.affine_select(out=v3, in_=v3, compare_op=ALU.is_ge, fill=0, base=2 * k - 1, pattern=[[2 * k, CH // (2 * k)], [0, 2 * k]], channel_multiplier=-1))
            link(g.memset(mt1[:], 1))
            v3 = mt1[:].rearrange("p (b e) -> p b e", e=2)
            link(g.memset(v3[:, :, 0], 0))
            for m in (1, -1):
                link(g.affine_select(out=v3, in_=v3, compare_op=ALU.is_ge, fill=0, base=0, pattern=[[-2 * m, CH // 2], [0, 2]], channel_multiplier=m))
            for m, base in ((mstrict, -1), (mincl, 0)):
                link(g.memset(m[:], 1))
                link(g.affine_select(out=m[:], in_=m[:], compare_op=ALU.is_ge, fill=0, base=base, pattern=[[1, CH]], channel_multiplier=-1))
            link(g.memset(keep[:], 1.0))
            link(g.memset(keep[:].rearrange("p (j c) -> p j c", c=NCC)[:, :, NCC - 1], 0.0))
            link(g.memset(restart[:], 1.0))
            link(g.memset(restart[:].rearrange("p (d t) -> p d t", d=NDIR)[:, :, 0], 0.0))
            link(g.memset(Sz[:], 0.0))
            link(g.memset(hmask[:], 0.0))
            for h in two:
                link(g.memset(hmask[hp(h), h:h + 1], 1.0))
            for s in two:
                link(g.memset(WTz[s][:], 0.0))
                for z in (AKT[s], RBT[s], RKT[s]):
                    link(g.memset(z[:], 0.0))
                for e in [M2[s], MT2[s]] + [TT[k][s] for k in LEVELS]:
                    for u in range(U):
                        g.tensor_copy(e[:, u, :], ident[:]).then_inc(init, 1)
            g.wait_ge(init, 2 * U * 8)

            def operands(n, it):
                for s in two:
                    g.wait_ge(cumr[s], n + 1)
                    if it is not None:
                        g.wait_ge(expr[s], n * 4)
                    g.tensor_tensor(cumx[s][:], cum[s][:], feat[s][:, 5], ALU.subtract).then_inc(cumxr[s], 1)
                for s in two:
                    g.wait_ge(expr[s], n * 4 + 4)
                    if it is not None:
                        done(g, s, it, "rkt")
                    for o, f, e in ((at, 2, 1), (bt, 1, 2), (kt, 0, 2)):
                        g.tensor_tensor(o[s][:], feat[s][:, f], ex[s][:, e], ALU.mult).then_inc(xp[s], 1)
                    g.wait_ge(xp[s], n * NXP + 3)
                    for o, oz in ((at, atz), (bt, btz), (kt, ktz)):
                        for h in two:
                            g.tensor_tensor(oz[s][:, h], o[s][:], hmask[:, h:h + 1].unsqueeze(1).broadcast_to([P, NDIR, CH]),
                                            ALU.mult).then_inc(xp[s], 1)

            operands(0, None)
            with g.Fori(0, NIT) as it:
                operands(it + 1, it)

        @block.sync
        def _(sp):
            for s in two:
                sp.dma_start(feat[s][:], fe_d[s]).then_inc(ld[s], 16)

            def next_load(it, n):
                for s in two:
                    sp.wait_ge(xp[s], it * NXP + NXP)
                    sp.wait_ge(rtr[s], it * 2 + 2)
                    done(sp, s, it, "tok2")
                    sp.dma_start(feat[s][:], fe_d[n * 2 + s]).then_inc(ld[s], 16)

            with sp.Fori(0, NIT - 1) as it:
                next_load(it, it + 1)
            next_load(NIT - 1, 0)
            for s in two:
                sp.wait_ge(ld[s], 16 * (NIT + 1))

        @block.scalar
        def _(act):
            def exps(n, first=False):
                for s in two:
                    act.wait_ge(cumr[s], n + 1)
                    if not first:
                        act.wait_ge(xp[s], n * NXP)
                        act.wait_ge(rtr[s], n * 2)
                    act.activation(ex[s][:, 0], cum[s][:], ACT.Exp, scale=-DECAY, bias=eps[:, 2:3]).then_inc(expr[s], 1)
                    act.activation(ex[s][:, 2], cum[s][:], ACT.Exp, scale=DECAY, bias=eps[:, 3:4]).then_inc(expr[s], 1)
                    act.activation(pc[s][:], cum[s][:, :, CH - 1], ACT.Exp, scale=-DECAY).then_inc(expr[s], 1)
                    act.wait_ge(cumxr[s], n + 1)
                    act.activation(ex[s][:, 1], cumx[s][:], ACT.Exp, scale=-DECAY, bias=eps[:, 2:3]).then_inc(expr[s], 1)

            exps(0, True)
            dst = {"at": AT, "tok1": TOK1, "tok2": TOK2, "lv": LV, "sa": SA, "mt64": MT}
            dst.update({f"m{k}": M for k in LEVELS if k < 64})

            def empty(s, it, name):
                done(act, s, it, name)
                if name == "y":
                    act.wait_ge(yst[s], it * 16)
                    act.activation(Y[s][:], ps[:, bank(s, name), 0:NDIR * CH].rearrange("p (d t) -> p d t", d=NDIR), ACT.Copy).then_inc(evA[s], 1)
                    emptied(act, s, it, "y")
                    act.dma_start(y_d[it * 2 + s], Y[s][:]).then_inc(yst[s], 16)
                else:
                    d = dst[name][s]
                    act.activation(d[:], psv(s, name, HD if name in ("lv", "sa") else CH), ACT.Copy).then_inc(evA[s], 1)

            with act.Fori(0, NIT) as it:
                for name in A_ORDER:
                    if name in ("sa", "y"):
                        continue
                    for s in two:
                        empty(s, it, name)
                    if name == "m16":
                        exps(it + 1)
                for s in two:
                    empty(s, it, "sa")
                    empty(s, it, "y")
            for s in two:
                act.wait_ge(yst[s], 16 * NIT)

        @block.vector
        def _(v):
            v.wait_ge(msk, 0)
            dst = {"a": (M2, ml[1]), "akt": (AKT, mstrict), "rbt": (RBT, mincl), "rkt": (RKT, mincl)}
            dst.update({f"t{k}": (TT[k], ml[k]) for k in LEVELS})

            def cumulate(n, first=False):
                for s in two:
                    v.wait_ge(ld[s], n * 16 + 16)
                    if not first:
                        v.wait_ge(expr[s], n * 4)
                    flat = lambda t: t.rearrange("p d t -> p (d t)")
                    v.tensor_tensor_scan(flat(cum[s][:]), restart[:], flat(feat[s][:, 5]), 0.0, ALU.mult, ALU.add).then_inc(cumr[s], 1)

            def r_operand(n, it=None):
                for s in two:
                    v.wait_ge(expr[s], n * 4 + 4)
                    if it is not None:
                        done(v, s, it, "y")
                    v.tensor_tensor(rt[s][:], feat[s][:, 3], ex[s][:, 0], ALU.mult).then_inc(rtr[s], 1)
                    if s == 0 or it is None:
                        v.tensor_copy(pcu[s][:], pc[s][:]).then_inc(rtr[s], 1)
                    else:
                        v.tensor_scalar(pcu[s][:], pc[s][:], keep[:, bass.ds(n, 1)], None, ALU.mult).then_inc(rtr[s], 1)

            def empty(s, it, name):
                if name == "mt2_init":
                    emptied(v, s, it, "at")
                    v.tensor_copy(tick[:, s * ND + D_ORDER.index(name):][:, 0:1], ident[:, 0:1])
                    v.copy_predicated(MT2[s][:], bc(mt1), AT[s][:]).then_inc(evD[s], 1)
                    return
                done(v, s, it, name)
                if name in dst:
                    t, m = dst[name]
                    v.tensor_copy(tick[:, s * ND + D_ORDER.index(name):][:, 0:1], ident[:, 0:1])
                    v.copy_predicated(t[s][:], bc(m), psv(s, name)).then_inc(evD[s], 1)
                elif name == "wt":
                    o = ps[:, bank(s, name), 0:NDIR * CH].rearrange("p (d t) -> p d t", d=NDIR)
                    for h in two:
                        v.tensor_copy(WTz[s][hp(h), h], o[hp(h)]).then_inc(evD[s], 1)
                elif name == "st":
                    o = ps[:, bank(s, name), 0:NDIR * HD].rearrange("p (d t) -> p d t", d=NDIR)
                    for h in two:
                        v.tensor_tensor(stmp[hp(h)], Sz[hp(h), h], o[hp(h)], ALU.add).then_inc(evD[s], 1)
                    emptied(v, s, it, "st")
                    for h in two:
                        v.tensor_tensor(Sz[hp(h), h], stmp[hp(h)], pcu[s][hp(h)].unsqueeze(2).broadcast_to([HD, NDIR, HD]), ALU.mult).then_inc(evD[s], 1)
                    emptied(v, s, it, "st_scaled")
                else:
                    v.tensor_copy(MT[s][:], psv(s, name)).then_inc(evD[s], 1)

            v.wait_ge(init, 2 * U * 8)
            v.wait_ge(msk, 4 * 7 + 4 + 4 + 5 + 3 + 2 * 4)
            cumulate(0, True)
            r_operand(0)
            with v.Fori(0, NIT) as it:
                for name in D_ORDER:
                    if name[:2] == "st" or name == "wt_head0":
                        continue
                    for s in two:
                        empty(s, it, name)
                    if name == "t8":
                        cumulate(it + 1)
                for s in two:
                    empty(s, it, "st")
                r_operand(it + 1, it)

        @block.tensor
        def _(pe):
            def bank_and_results(s, it, name, reads):
                prev = STEPS.index(name) - 4
                names = ([STEPS[prev]] if prev >= 0 else []) + list(reads)
                a = max([A_ORDER.index(x) + 1 for x in names if x in A_ORDER] + [0])
                d = max([D_ORDER.index(x) + 1 for x in names if x in D_ORDER] + [0])
                if a or prev < 0:
                    pe.wait_ge(evA[s], it * NA + a)
                if d or prev < 0:
                    pe.wait_ge(evD[s], it * ND + d)

            def step(s, it, name, waits, mms):
                bank_and_results(s, it, name, waits)
                for out, l, r, st, sp_ in mms:
                    mm = pe.matmul(out, l, r, start=st, stop=sp_)
                mm.then_inc(pes[s], 1)

            def gram(s, it, name, L, R, waits=()):
                o = psv(s, name)
                step(s, it, name, waits, [(o[:, u, :], L[s][:, h, d, :], R[s][:, d, :], True, True) for u, (d, h) in enumerate(units)])

            def full(s, it, name, L, R, waits):
                o = psv(s, name)
                step(s, it, name, waits, [(o[:, u, :], L[s][:, u, :], R[s][:, u, :], True, True) for u in range(U)])

            def tr(s, it, name, pair):
                o = psv(s, name)
                bank_and_results(s, it, name, [])
                for q, src in enumerate(pair):
                    mm = pe.transpose(o[:, q, :], src, ident[:])
                mm.then_inc(pes[s], 1)

            def one(s, it, name):
                if name == "at":
                    pe.wait_ge(xp[s], it * NXP + NXP)
                    gram(s, it, name, btz, at)
                elif name == "a":
                    gram(s, it, name, atz, bt)
                elif name == "akt":
                    gram(s, it, name, ktz, at)
                elif name == "tok1":
                    tr(s, it, name, [at[s][:, 0], at[s][:, 1], bt[s][:, 0], bt[s][:, 1]])
                elif name == "tok2":
                    tr(s, it, name, [kt[s][:, 0], kt[s][:, 1], feat[s][:, 4, 0], feat[s][:, 4, 1]])
                elif name == "rbt":
                    pe.wait_ge(rtr[s], it * 2 + 2)
                    gram(s, it, name, btz, rt)
                elif name == "rkt":
                    gram(s, it, name, ktz, rt)
                elif name == "t2":
                    full(s, it, name, AT, M2, ["at", "a"])
                elif name == "m2":
                    full(s, it, name, MT2, TT[2], ["mt2_init", "t2"])
                elif name == "mt2":
                    full(s, it, name, TT[2], MT2, [])
                elif name == "lv":
                    o = psv(s, name, HD)
                    step(s, it, name, ["akt", "tok2"], [(o[:, u, :], AKT[s][:, u, :], TOK2[s][:, 2 + d, hp(h)], True, True) for u, (d, h) in enumerate(units)])
                elif name[0] == "t":
                    k = int(name[1:])
                    full(s, it, name, AT, M, [f"m{k // 2}"])
                elif name[:2] == "mt":
                    k = int(name[2:])
                    full(s, it, name, TT[k], MT, [f"mt{k // 2}", f"t{k}"])
                elif name[0] == "m":
                    k = int(name[1:])
                    full(s, it, name, MT, TT[k], [f"mt{k // 2}", f"t{k}"])
                elif name == "wt":
                    o = ps[:, bank(s, name), 0:NDIR * CH].rearrange("p (d t) -> p d t", d=NDIR)
                    step(s, it, name, ["mt64", "tok1"], [(o[hp(h), d, :], TOK1[s][:, d, hp(h)], MT[s][:, u, :], True, True) for u, (d, h) in enumerate(units)])
                elif name == "sa":
                    o = psv(s, name, HD)
                    mms = []
                    for u, (d, h) in enumerate(units):
                        mms += [(o[:, u, :], MT[s][:, u, :], LV[s][:, u, :], True, False),
                                (o[:, u, :], WTz[s][:, h, d, :], Sz[:, h, d, :], False, True)]
                    if s == 0:
                        pe.wait_ge(evD[1], it * ND)
                    else:
                        emptied(pe, 0, it, "st_scaled")
                    step(s, it, name, ["lv", "wt"], mms)
                elif name == "y":
                    o = ps[:, bank(s, name), 0:NDIR * CH].rearrange("p (d t) -> p d t", d=NDIR)
                    mms = []
                    for u, (d, h) in enumerate(units):
                        mms += [(o[hp(h), d, :], TOK2[s][:, 2 + d, hp(h)], RKT[s][:, u, :], True, False),
                                (o[hp(h), d, :], Sz[:, h, d, :], rt[s][:, d, :], False, False),
                                (o[hp(h), d, :], SA[s][:, u, :], RBT[s][:, u, :], False, True)]
                    step(s, it, name, ["sa", "rkt", "rbt"], mms)
                elif name == "st":
                    o = ps[:, bank(s, name), 0:NDIR * HD].rearrange("p (d t) -> p d t", d=NDIR)
                    mms = []
                    for u, (d, h) in enumerate(units):
                        mms += [(o[hp(h), d, :], TOK2[s][:, d, hp(h)], TOK2[s][:, 2 + d, hp(h)], True, False),
                                (o[hp(h), d, :], TOK1[s][:, 2 + d, hp(h)], SA[s][:, u, :], False, True)]
                    step(s, it, name, ["sa"], mms)

            pe.wait_ge(init, 2 * U * 8)
            with pe.Fori(0, NIT) as it:
                for name in STEPS:
                    if name in ("sa", "y", "st"):
                        continue
                    for s in two:
                        one(s, it, name)
                for s in two:
                    for name in ("sa", "y", "st"):
                        one(s, it, name)
    ph.close()


def kernel(x, c, ctx, c_ctx, mod_w, mod_b, norm_pre, norm_post, f_w_in, f_w_mix, f_b_mix, f_w_out,
           r_mu, r_w_in, r_w0, r_w1, r_w2, r_a0, r_a1, r_a2, r_v0, r_v1, r_v2,
           r_k_k, r_k_a, r_r_k, r_ln_w, r_ln_b, r_w_out):
    import concourse.bacc as bacc
    from concourse.bass_utils import run_bass_kernel_spmd

    n = lambda a: np.asarray(a)
    cols = lambda a: n(a).reshape(-1, P).T
    slabs = lambda w, e: np.ascontiguousarray(n(w).reshape(KT, P, e, P).transpose(2, 1, 0, 3))
    vec = np.ascontiguousarray(np.concatenate([cols(a) for a in (
        c, c_ctx, n(mod_b)[0], n(mod_b)[1], norm_pre, norm_post, f_b_mix, r_mu, r_w0, r_a0, r_k_k, r_k_a, r_r_k, r_ln_w, r_ln_b)], axis=1))
    ang = lambda a, b, m: 2 * np.pi * ((np.outer(np.arange(a), np.arange(b)) % m) / m)
    cg = ang(P, P, P)
    ctab = np.stack([np.cos(cg), np.sin(cg)], axis=1) / np.sqrt(P)
    tg = ang(LAT, HALF, LAT).reshape(KT, P, HALF)
    tlat = np.stack([np.cos(tg), np.sin(tg)], axis=2).transpose(1, 0, 2, 3) / np.sqrt(LAT)
    alt = np.stack([(-1.0) ** np.arange(P)] * 2, axis=1) / np.sqrt(LAT)
    xg = ang(CTX, CTX, CTX).reshape(2, P, CTX)
    tctx = np.stack([np.cos(xg), -np.sin(xg)], axis=2).transpose(1, 0, 2, 3) / np.sqrt(CTX)
    f = lambda a: np.ascontiguousarray(a.astype(np.float32))
    up = lambda w: n(w).reshape(NDIR * LORA, KT, P).transpose(1, 0, 2)
    down = lambda w: np.ascontiguousarray(n(w).reshape(NDIR, KT, P, LORA).transpose(2, 1, 0, 3).reshape(P, KT, P))
    arrays = {
        "vec": vec,
        "xt": np.ascontiguousarray(np.concatenate([n(ctx)[0], n(x)[0]], axis=0).T.reshape(KT, P, T)),
        "modw": np.ascontiguousarray(n(mod_w).reshape(2, KT, P, 24, P).transpose(0, 3, 2, 1, 4).reshape(48, P, KT, P)),
        "fwin": slabs(n(f_w_in)[0], 2 * KT), "fwout": slabs(n(f_w_out)[0], KT), "rwout": slabs(n(r_w_out)[0], KT),
        "rwin": np.concatenate([slabs(n(r_w_in)[0, i], KT) for i in range(4)], axis=0),
        "wmix": np.ascontiguousarray(n(f_w_mix)[0].transpose(1, 0, 2)),
        "ctab": f(ctab), "tlat": f(tlat), "alt": f(alt), "tctx": f(tctx),
        "w1": down(n(r_w1)[0]), "a1": down(n(r_a1)[0]),
        "w2a2": np.ascontiguousarray(np.stack([up(n(r_w2)[0]), up(n(r_a2)[0])], axis=2)),
    }
    nc = bacc.Bacc("TRN2", target_bir_lowering=False, num_devices=1)
    A = {k: nc.dram_tensor(f"in_{k}", a.shape, F32, kind="ExternalInput").ap() for k, a in arrays.items()}
    A["out"] = nc.dram_tensor("out", [KT, P, LAT], F32, kind="ExternalOutput").ap()
    build(nc, A)
    r = run_bass_kernel_spmd(nc, [{f"in_{k}": a for k, a in arrays.items()}], core_ids=[0])
    return r.results[0]["out"].reshape(D, LAT).T[None]
```

```python
from contextlib import ExitStack

import numpy as np

import concourse.bass as bass
from concourse import mybir

F32 = mybir.dt.float32
I32 = mybir.dt.int32
ALU = mybir.AluOpType
ACT = mybir.ActivationFunctionType

P = 128
D = 1024
KT = D // P
CTX = 256
LAT = 1024
T = CTX + LAT
HD = 64
LORA = 64
NDIR = 2
CH = 128
NCH = T // CH
FG = P
HALF = LAT // 2
BLK = [(0, 512), (512, 512), (1024, 256)]
RMS_EPS = 1e-6
GN_EPS = 64e-5
DECAY = float(np.exp(-0.5))
SHIFT = DECAY * CH / 2

VEC = {}
for _n, _k in (("c", 1), ("c_ctx", 1), ("mod_b0", 3), ("mod_b1", 3), ("norm_pre", 2), ("norm_post", 2),
               ("f_b_mix", 1), ("mu", 6), ("w0", 2), ("a0", 2), ("k_k", 1), ("k_a", 1), ("r_k", 1),
               ("ln_w", 1), ("ln_b", 1)):
    VEC[_n] = sum(v[1] for v in VEC.values()) if VEC else 0
    VEC[_n] = (VEC[_n], _k * KT)
NVEC = sum(v[1] for v in VEC.values())

FEATS = ("kd", "b", "negkk", "r", "v", "sw")
NF = len(FEATS)


def lat(a):
    return slice(CTX + a, CTX + LAT)


def build(nc, A):
    es = ExitStack()
    with es:
        def sem(name):
            return es.enter_context(nc.semaphore(name))

        def dram(name, shape):
            return nc.dram_tensor(name, shape, F32, kind="Internal").ap()

        x1_d = dram("x1_scratch", [P, KT, LAT])
        sa_d = dram("iclr_scratch", [KT, P, NDIR, T])
        ks_d = dram("ksum_scratch", [KT, P, LAT])
        bv_d = dram("bonus_scratch", [KT, P, LAT])
        gz_d = dram("gate_scratch", [KT, P, LAT])
        fe_d = dram("feature_scratch", [KT * NCH, P, NF, NDIR, CH])
        y_d = dram("y_scratch", [KT * NCH, P, NDIR, CH])
        fe_v = fe_d.rearrange("(j c) p f d t -> j p f d c t", c=NCH)
        y_v = y_d.rearrange("(j c) p d t -> j p d c t", c=NCH)

        ps = es.enter_context(nc.psum_tensor("ps", [P, 8, 512], F32))
        vec = es.enter_context(nc.sbuf_tensor("vec", [P, NVEC], F32))
        mod = es.enter_context(nc.sbuf_tensor("mod", [P, 2, 24, 2], F32))
        pre_s = es.enter_context(nc.sbuf_tensor("pre_s", [P, 2, KT, 2], F32))
        post_s = es.enter_context(nc.sbuf_tensor("post_s", [P, 2, KT, 2], F32))
        ones = es.enter_context(nc.sbuf_tensor("ones", [P, P], F32))
        hones = es.enter_context(nc.sbuf_tensor("hones", [P, P], F32))
        ident = es.enter_context(nc.sbuf_tensor("ident", [P, P], F32))
        eps = es.enter_context(nc.sbuf_tensor("eps", [P, 4], F32))
        kam = es.enter_context(nc.sbuf_tensor("kam", [P, KT], F32))
        nkk = es.enter_context(nc.sbuf_tensor("nkk", [P, KT], F32))
        const_ready = sem("const_ready")

        def vcol(name, i, n=1):
            return vec[:, bass.ds(VEC[name][0] + i, n)]

        with ExitStack() as ph:
            wm = ph.enter_context(nc.sbuf_tensor("mod_slab", [P, 4, KT, P], F32))
            cond = ph.enter_context(nc.sbuf_tensor("cond", [P, KT, 2], F32))
            sig = ph.enter_context(nc.sbuf_tensor("cond_sig", [P, 2 * KT], F32))
            vec_in, slab_in = sem("vec_in"), [sem(f"mod_slab_in{i}") for i in range(4)]
            cond_ready, mod_mm, mod_out, cst, vchain = sem("cond_ready"), sem("mod_mm"), sem("mod_out"), sem("cst"), sem("mod_chain")
            cond_sig = sem("cond_sig_ready")
            NS = 48
            with nc.Block() as block:
                @block.sync
                def _(sp):
                    sp.dma_start(vec[:], A["vec"]).then_inc(vec_in, 16)
                    for s in range(4):
                        sp.dma_start(wm[:, s], A["modw"][s]).then_inc(slab_in[s], 16)
                    with sp.Fori(1, NS // 4) as i:
                        for s in range(4):
                            sp.wait_ge(mod_mm, i * 4 + (s - 3))
                            sp.dma_start(wm[:, s], A["modw"][i * 4 + s]).then_inc(slab_in[s], 16)

                @block.gpsimd
                def _(g):
                    g.memset(ones[:], 1.0).then_inc(cst, 1)
                    g.memset(ident[:], 0.0).then_inc(cst, 1)
                    g.memset(hones[:], 0.0).then_inc(cst, 1)
                    g.memset(eps[:, 0:1], RMS_EPS).then_inc(cst, 1)
                    g.memset(eps[:, 1:2], GN_EPS).then_inc(cst, 1)
                    g.memset(eps[:, 2:3], SHIFT).then_inc(cst, 1)
                    g.memset(eps[:, 3:4], -SHIFT).then_inc(cst, 1)
                    g.wait_ge(cst, 7)
                    g.affine_select(out=ident[:], in_=ident[:], compare_op=ALU.not_equal, fill=1.0, base=0,
                                    pattern=[[-1, P]], channel_multiplier=1).then_inc(cst, 1)
                    g.wait_ge(cst, 8)
                    g.memset(hones[0:HD, 0:HD], 1.0).then_inc(cst, 1)
                    g.wait_ge(cst, 9)
                    g.memset(hones[HD:P, HD:P], 1.0).then_inc(cst, 1)

                @block.scalar
                def _(act):
                    act.wait_ge(vec_in, 16)
                    act.activation(sig[:], vec[:, 0:2 * KT], ACT.Sigmoid).then_inc(cond_sig, 1)

                @block.vector
                def _(v):
                    n = [0]

                    def link(ins):
                        n[0] += 1
                        ins.then_inc(vchain, 1)
                        v.wait_ge(vchain, n[0])

                    v.wait_ge(vec_in, 16)
                    link(v.tensor_scalar(kam[:], vcol("k_a", 0, KT), -1.0, 1.0, ALU.mult, ALU.add))
                    link(v.tensor_scalar(nkk[:], vcol("k_k", 0, KT), -1.0, None, ALU.mult))
                    v.wait_ge(cond_sig, 1)
                    v.tensor_tensor(cond[:].rearrange("p k c -> p c k"), vec[:, 0:2 * KT].rearrange("p (c k) -> p c k", c=2),
                                    sig[:].rearrange("p (c k) -> p c k", c=2), ALU.mult).then_inc(cond_ready, 1)
                    mf = mod[:].rearrange("p l m c -> p (l m) c")
                    with v.Fori(0, NS // 2) as i:
                        for s in range(2):
                            v.wait_ge(mod_mm, i * 2 + (s + 1))
                            v.tensor_copy(mf[:, i * 2 + s, :], ps[:, s, 0:2]).then_inc(mod_out, 1)
                    v.wait_ge(mod_out, NS)
                    for c in range(2):
                        link(v.tensor_tensor(mod[:, :, :, c], mod[:, :, :, c],
                                             vec[:, VEC["mod_b0"][0]:VEC["mod_b0"][0] + NS].rearrange("p (l m) -> p l m", l=2), ALU.add))
                    for c in range(2):
                        link(v.scalar_tensor_tensor(pre_s[:, :, :, c], mod[:, :, KT:2 * KT, c], 1.0,
                                                    vcol("norm_pre", 0, 2 * KT).rearrange("p (l k) -> p l k", l=2), ALU.add, ALU.mult))
                        link(v.tensor_tensor(post_s[:, :, :, c], mod[:, :, 2 * KT:3 * KT, c],
                                             vcol("norm_post", 0, 2 * KT).rearrange("p (l k) -> p l k", l=2), ALU.mult))

                @block.tensor
                def _(pe):
                    pe.wait_ge(cond_ready, 1)
                    with pe.Fori(0, NS // 4) as i:
                        for s in range(4):
                            pe.wait_ge(slab_in[s], i * 16 + 16)
                            pe.wait_ge(mod_out, i * 4 + (s - 1 if s >= 2 else 0))
                            for k in range(KT):
                                mm = pe.matmul(ps[:, s % 2, 0:2], wm[:, s, k, :], cond[:, k, :], start=k == 0, stop=k == KT - 1)
                            mm.then_inc(mod_mm, 1)

        stat_sems = {n: sem(n) for n in ("sq_ready", "sq_used", "sum_ready", "root", "rstd_ready")}
        stat_base = {n: 0 for n in stat_sems}

        def rms_stats(ph, tag, src, ntok, loads=None):
            blks = [(a, min(512, ntok - a)) for a in range(0, ntok, 512)]
            sq = ph.enter_context(nc.sbuf_tensor(f"sq_{tag}", [P, 2, ntok], F32))
            rstd = ph.enter_context(nc.sbuf_tensor(f"rstd_{tag}", [P, ntok], F32))
            s, base = stat_sems, dict(stat_base)
            for n, count in (("sq_ready", KT), ("sq_used", KT), ("sum_ready", 1), ("root", len(blks)), ("rstd_ready", 1)):
                stat_base[n] += count

            def scalar(act, ready):
                for k in range(KT):
                    ready(act, k)
                    if k >= 2:
                        act.wait_ge(s["sq_used"], base["sq_used"] + (k - 1))
                    act.activation(sq[:, k % 2, :], src(k), ACT.Square).then_inc(s["sq_ready"], 1)
                act.wait_ge(s["sum_ready"], base["sum_ready"] + 1)
                for b, (a, n) in enumerate(blks):
                    act.activation(rstd[:, a:a + n], ps[:, b, 0:n], ACT.Sqrt, scale=1.0 / D, bias=eps[:, 0:1]).then_inc(s["root"], 1)

            def tensor(pe):
                for k in range(KT):
                    pe.wait_ge(s["sq_ready"], base["sq_ready"] + (k + 1))
                    for b, (a, n) in enumerate(blks):
                        mm = pe.matmul(ps[:, b, 0:n], ones[:], sq[:, k % 2, a:a + n], start=k == 0, stop=k == KT - 1)
                    mm.then_inc(s["sq_used"], 1)
                pe.matmul(ps[:, 7, 0:2], ones[:], ones[:, 0:2], start=True, stop=True).then_inc(s["sum_ready"], 1)

            def vector(v):
                v.wait_ge(s["root"], base["root"] + len(blks))
                v.reciprocal(rstd[:], rstd[:]).then_inc(s["rstd_ready"], 1)
                v.wait_ge(s["rstd_ready"], base["rstd_ready"] + 1)

            return rstd, s["rstd_ready"], scalar, tensor, vector

        def pre_norm(v, act, layer, src, rstd, rstd_ready, xn, xn_ready, h, h_ready, spill=None):
            if v is not None:
                for k in range(KT):
                    if k >= 2:
                        v.wait_ge(h_ready, 2 * (k - 1))
                    v.tensor_tensor(xn[:, k % 2, :], src(k), rstd[:], ALU.mult).then_inc(xn_ready, 1)
            else:
                for k in range(KT):
                    act.wait_ge(xn_ready, k + 1)
                    for c, seg in ((1, slice(0, CTX)), (0, slice(CTX, T))):
                        act.activation(h[:, k, seg], xn[:, k % 2, seg], ACT.Identity,
                                       scale=pre_s[:, layer, k, c:c + 1], bias=mod[:, layer, k, c:c + 1]).then_inc(h_ready, 1)

        l0 = es.enter_context(ExitStack())
        xt = l0.enter_context(nc.sbuf_tensor("xt", [P, KT, T], F32))
        fgo = l0.enter_context(nc.sbuf_tensor("fgo", [P, KT, T], F32))
        h0 = l0.enter_context(nc.sbuf_tensor("h0", [P, KT, T], F32))
        with ExitStack() as ph:
            x_in = [sem(f"x_in{i}") for i in range(2)]
            xn = ph.enter_context(nc.sbuf_tensor("xn0", [P, 2, T], F32))
            xn_ready, h_ready = sem("xn0_ready"), sem("h0_ready")
            rstd, rr, f_act, f_pe, f_dve = rms_stats(ph, "pre0", lambda k: xt[:, k, :], T)
            with nc.Block() as block:
                @block.sync
                def _(sp):
                    for i in range(2):
                        ks = slice(i * KT // 2, (i + 1) * KT // 2)
                        sp.dma_start(xt[:, ks, :], A["xt"][ks].rearrange("k p t -> p k t")).then_inc(x_in[i], 16)

                @block.scalar
                def _(act):
                    f_act(act, lambda e, k: e.wait_ge(x_in[k // (KT // 2)], 16))
                    pre_norm(None, act, 0, None, None, None, xn, xn_ready, h0, h_ready)

                @block.tensor
                def _(pe):
                    f_pe(pe)

                @block.vector
                def _(v):
                    for i in range(2):
                        v.wait_ge(x_in[i], 16)
                    f_dve(v)
                    pre_norm(v, None, 0, lambda k: xt[:, k, :], rstd, rr, xn, xn_ready, h0, h_ready)

        with ExitStack() as ph:
            def sb(name, shape):
                return ph.enter_context(nc.sbuf_tensor(name, shape, F32))
            wi = sb("fw_slab", [P, 2, KT, P])
            ctab = sb("ctab", [P, 2, P])
            wmx = sb("wmix", [P, KT, P])
            cw = sb("cw", [P, KT, 2 * P])
            tl = sb("time_tab_lat", [P, KT, 2, HALF])
            alt = sb("alt", [P, 2])
            tc = sb("time_tab_ctx", [P, 2, 2, CTX])
            ub = sb("u_group", [P, T])
            zb = sb("z_group", [P, 1, T])
            ab = sb("ab_group", [P, NCH, 2 * P])
            qs = sb("q_part", [P, HALF])
            fb = sb("f_group", [P, T])
            tab_in, w_in_u, w_in_z = sem("tab_in"), sem("w_in_u"), sem("w_in_z")
            cwp, cwr = sem("cw_products"), sem("cw_ready")
            u_mm, z_mm, ab_mm, f_mm = sem("u_mm"), sem("z_mm"), sem("ab_mm"), sem("f_mm")
            u_out, zs_out, ab_out, q_out, f_out, fg_out, z_out = (sem("u_out"), sem("zs_out"), sem("ab_out"), sem("q_out"), sem("f_out"),
                                                                  sem("fg_out"), sem("z_out"))
            zsig = zb[:, 0, :]
            with nc.Block() as block:
                @block.sync
                def _(sp):
                    sp.dma_start(ctab[:], A["ctab"]).then_inc(tab_in, 16)
                    sp.dma_start(wmx[:], A["wmix"]).then_inc(tab_in, 16)
                    sp.dma_start(tl[:], A["tlat"]).then_inc(tab_in, 16)
                    sp.dma_start(alt[:], A["alt"]).then_inc(tab_in, 16)
                    sp.dma_start(tc[:], A["tctx"]).then_inc(tab_in, 16)
                    sp.dma_start(wi[:, 0], A["fwin"][0]).then_inc(w_in_u, 16)
                    sp.dma_start(wi[:, 1], A["fwin"][KT]).then_inc(w_in_z, 16)
                    with sp.Fori(1, KT) as g:
                        sp.wait_ge(u_mm, g * 3)
                        sp.dma_start(wi[:, 0], A["fwin"][g]).then_inc(w_in_u, 16)
                        sp.wait_ge(z_mm, g * 3)
                        sp.dma_start(wi[:, 1], A["fwin"][g + KT]).then_inc(w_in_z, 16)

                @block.tensor
                def _(pe):
                    pe.wait_ge(tab_in, 80)
                    for g in range(KT):
                        if g >= 4:
                            pe.wait_ge(cwr, g - 3)
                        for c in range(2):
                            mm = pe.matmul(ps[:, g % 4, c * P:c * P + P], ctab[:, c, :], wmx[:, g, :], start=True, stop=True)
                        mm.then_inc(cwp, 1)
                    pe.wait_ge(cwr, KT)
                    with pe.Fori(0, KT) as g:
                        for half, win, done, b0 in ((0, w_in_u, u_mm, 0), (1, w_in_z, z_mm, 3)):
                            pe.wait_ge(win, g * 16 + 16)
                            if half == 0:
                                pe.wait_ge(ab_out, g * 5)
                            else:
                                pe.wait_ge(f_out, g * 4)
                            for b, (a, n) in enumerate(BLK):
                                for k in range(KT):
                                    mm = pe.matmul(ps[:, b0 + b, 0:n], wi[:, half, k, :], h0[:, k, a:a + n], start=k == 0, stop=k == KT - 1)
                                mm.then_inc(done, 1)
                        pe.wait_ge(u_out, g * 3 + 3)
                        for q in range(NCH // 2):
                            for t in range(2):
                                mm = pe.matmul(ps[:, (6 + q) % 8, t * 256:t * 256 + 256], ub[:, (2 * q + t) * P:(2 * q + t + 1) * P],
                                               cw[:, g, :], start=True, stop=True)
                            mm.then_inc(ab_mm, 1)
                        pe.wait_ge(z_out, g * 3 + 3)
                        pe.wait_ge(ab_out, g * 5 + 5)
                        for c in range(2):
                            for t in range(KT):
                                mm = pe.matmul(ps[:, 3 + c, :], ab[:, 2 + t, c * P:c * P + P], tl[:, t, c, :], start=t == 0, stop=t == KT - 1)
                            mm.then_inc(f_mm, 1)
                        for t in range(KT):
                            mm = pe.matmul(ps[:, 5, CTX:CTX + 2], ab[:, 2 + t, 0:P], alt[:], start=t == 0, stop=t == KT - 1)
                        for c in range(2):
                            for t in range(2):
                                mm = pe.matmul(ps[:, 5, 0:CTX], ab[:, t, c * P:c * P + P], tc[:, t, c, :],
                                               start=c + t == 0, stop=c + t == 2)
                        mm.then_inc(f_mm, 1)

                @block.scalar
                def _(act):
                    for g in range(KT):
                        act.wait_ge(cwp, g + 1)
                        act.activation(cw[:, g, :], ps[:, g % 4, 0:2 * P], ACT.Copy).then_inc(cwr, 1)
                    act.wait_ge(cwr, KT)
                    with act.Fori(0, KT) as g:
                        for b, (a, n) in enumerate(BLK):
                            act.wait_ge(u_mm, g * 3 + (b + 1))
                            if b == 0:
                                act.wait_ge(ab_mm, g * 5)
                            act.activation(ub[:, a:a + n], ps[:, b, 0:n], ACT.Copy).then_inc(u_out, 1)
                        for b, (a, n) in enumerate(BLK):
                            act.wait_ge(z_mm, g * 3 + (b + 1))
                            if b == 0:
                                act.wait_ge(fg_out, g)
                            act.activation(zsig[:, a:a + n], ps[:, 3 + b, 0:n], ACT.Sigmoid).then_inc(zs_out, 1)
                        act.wait_ge(f_mm, g * 3 + 2)
                        act.activation(qs[:], ps[:, 4, :], ACT.Copy).then_inc(q_out, 1)

                @block.vector
                def _(v):
                    with v.Fori(0, KT) as g:
                        for b, (a, n) in enumerate(BLK):
                            v.wait_ge(zs_out, g * 3 + (b + 1))
                            v.tensor_tensor(zb[:, 0, a:a + n], zsig[:, a:a + n], ps[:, 3 + b, 0:n], ALU.mult).then_inc(z_out, 1)
                        for q in range(NCH // 2):
                            v.wait_ge(ab_mm, g * 5 + (q + 1))
                            v.tensor_copy(ab[:, 2 * q:2 * q + 2, :], ps[:, (6 + q) % 8, :].rearrange("p (t e) -> p t e", t=2)).then_inc(ab_out, 1)
                        v.wait_ge(f_mm, g * 3 + 3)
                        v.tensor_copy(fb[:, 0:CTX], ps[:, 5, 0:CTX]).then_inc(f_out, 1)
                        v.tensor_copy(fb[:, CTX + HALF:CTX + HALF + 1], ps[:, 5, CTX:CTX + 1]).then_inc(f_out, 1)
                        v.wait_ge(q_out, g + 1)
                        v.tensor_tensor(fb[:, CTX:CTX + HALF], ps[:, 3, :], qs[:], ALU.subtract).then_inc(f_out, 1)
                        v.tensor_tensor(fb[:, CTX + HALF + 1:T][:, ::-1], ps[:, 3, 1:HALF], qs[:, 1:HALF], ALU.add).then_inc(f_out, 1)
                        v.wait_ge(f_out, g * 4 + 4)
                        v.scalar_tensor_tensor(fgo[:, g, :], fb[:], vec[:, bass.ds(g + VEC["f_b_mix"][0], 1)], zb[:, 0, :],
                                               ALU.add, ALU.mult).then_inc(fg_out, 1)

        def out_proj(ph, tag, wts, src, dst, ntok):
            blks = [(a, min(512, ntok - a)) for a in range(0, ntok, 512)]
            nb = len(blks)
            w = ph.enter_context(nc.sbuf_tensor(f"wo_{tag}", [P, 2, KT, P], F32))
            w_in = [sem(f"wo_in{i}_{tag}") for i in range(2)]
            mm_done, out_done = sem(f"o_mm_{tag}"), sem(f"o_out_{tag}")
            with nc.Block() as block:
                @block.sync
                def _(sp):
                    for s in range(2):
                        sp.dma_start(w[:, s], wts[s]).then_inc(w_in[s], 16)
                    with sp.Fori(1, KT // 2) as i:
                        for s in range(2):
                            sp.wait_ge(mm_done, i * (2 * nb) + (s - 1) * nb)
                            sp.dma_start(w[:, s], wts[i * 2 + s]).then_inc(w_in[s], 16)

                @block.tensor
                def _(pe):
                    with pe.Fori(0, KT // 2) as i:
                        for s in range(2):
                            pe.wait_ge(w_in[s], i * 16 + 16)
                            for b, (a, n) in enumerate(blks):
                                if s == 1:
                                    pe.wait_ge(out_done, i * (2 * nb) + (b + 1))
                                else:
                                    pe.wait_ge(out_done, i * (2 * nb) )
                                for k in range(KT):
                                    mm = pe.matmul(ps[:, b, 0:n], w[:, s, k, :], src[:, k, a:a + n], start=k == 0, stop=k == KT - 1)
                                mm.then_inc(mm_done, 1)

                @block.scalar
                def _(act):
                    with act.Fori(0, KT // 2) as i:
                        for s in range(2):
                            for b, (a, n) in enumerate(blks):
                                act.wait_ge(mm_done, i * (2 * nb) + (s * nb + b + 1))
                                act.activation(dst[:, i * 2 + s, a:a + n], ps[:, b, 0:n], ACT.Copy).then_inc(out_done, 1)

        with ExitStack() as ph:
            out_proj(ph, "l0", A["fwout"], fgo, h0, T)

        with ExitStack() as ph:
            rstd, rr, f_act, f_pe, f_dve = rms_stats(ph, "post0", lambda k: h0[:, k, :], T)
            on = ph.enter_context(nc.sbuf_tensor("on0", [P, 2, T], F32))
            on_ready, x_ready, on_chain = sem("on0_ready"), sem("x1_ready"), sem("on0_chain")
            with nc.Block() as block:
                @block.scalar
                def _(act):
                    f_act(act, lambda e, k: None)

                @block.tensor
                def _(pe):
                    f_pe(pe)

                @block.vector
                def _(v):
                    f_dve(v)
                    for k in range(KT):
                        if k >= 2:
                            v.wait_ge(x_ready, 2 * (k - 1))
                        v.tensor_tensor(on[:, k % 2, :], h0[:, k, :], rstd[:], ALU.mult).then_inc(on_ready, 1)
                        v.wait_ge(on_ready, k + 1)
                        for c, seg in ((1, slice(0, CTX)), (0, slice(CTX, T))):
                            v.scalar_tensor_tensor(xt[:, k, seg], on[:, k % 2, seg], post_s[:, 0, k, c:c + 1], xt[:, k, seg],
                                                   ALU.mult, ALU.add).then_inc(x_ready, 1)
        with ExitStack() as ph:
            xn = ph.enter_context(nc.sbuf_tensor("xn1", [P, 2, T], F32))
            xn_ready, h_ready, spill = sem("xn1_ready"), sem("h1_ready"), sem("x1_spilled")
            rstd, rr, f_act, f_pe, f_dve = rms_stats(ph, "pre1", lambda k: xt[:, k, :], T)
            with nc.Block() as block:
                @block.sync
                def _(sp):
                    sp.dma_start(x1_d, xt[:, :, CTX:T]).then_inc(spill, 16)
                    sp.wait_ge(spill, 16)

                @block.scalar
                def _(act):
                    f_act(act, lambda e, k: None)
                    pre_norm(None, act, 1, None, None, None, xn, xn_ready, h0, h_ready)

                @block.tensor
                def _(pe):
                    f_pe(pe)

                @block.vector
                def _(v):
                    f_dve(v)
                    pre_norm(v, None, 1, lambda k: xt[:, k, :], rstd, rr, xn, xn_ready, h0, h_ready)

        GW = 64
        with ExitStack() as ph:
            nb_ = ph.enter_context(nc.sbuf_tensor("neighbours", [P, 2, T], F32))
            sc_, sd = sem("shift_chain"), sem("shift_done")
            pc_ = sem("shift_pool")
            with nc.Block() as block:
                @block.vector
                def _(v):
                    n = [0]

                    def link(ins):
                        n[0] += 1
                        ins.then_inc(sc_, 1)
                        v.wait_ge(sc_, n[0])

                    for k in range(KT):
                        s = nb_[:, k % 2, :]
                        h = h0[:, k, :]
                        sl, hl = s[:, CTX:T], h[:, CTX:T]
                        sg = sl.rearrange("p (r w) -> p r w", w=GW)
                        hg = hl.rearrange("p (r w) -> p r w", w=GW)
                        link(v.tensor_tensor(sl[:, GW:LAT - GW], hl[:, 0:LAT - 2 * GW], hl[:, 2 * GW:LAT], ALU.add))
                        link(v.tensor_copy(sl[:, 0:GW], hl[:, GW:2 * GW]))
                        link(v.tensor_copy(sl[:, LAT - GW:LAT], hl[:, LAT - 2 * GW:LAT - GW]))
                        link(v.tensor_tensor(sg[:, :, 1:GW], sg[:, :, 1:GW], hg[:, :, 0:GW - 1], ALU.add))
                        link(v.tensor_tensor(sg[:, :, 0:GW - 1], sg[:, :, 0:GW - 1], hg[:, :, 1:GW], ALU.add))
                        link(v.scalar_tensor_tensor(fgo[:, k, CTX:T], sl, 0.25, hl, ALU.mult, ALU.subtract))
                        link(v.tensor_tensor(s[:, 1:CTX - 1], h[:, 0:CTX - 2], h[:, 2:CTX], ALU.add))
                        link(v.tensor_copy(s[:, 0:1], h[:, 1:2]))
                        link(v.tensor_copy(s[:, CTX - 1:CTX], h[:, CTX - 2:CTX - 1]))
                        link(v.scalar_tensor_tensor(fgo[:, k, 0:CTX], s[:, 0:CTX], 0.5, h[:, 0:CTX], ALU.mult, ALU.subtract))

        dl, h1 = fgo, h0

        def mix(ph, tag, m, lo):
            done = sem(f"mixed_{tag}")

            def vector(v):
                for k in range(KT):
                    v.scalar_tensor_tensor(xt[:, k, lo:T], dl[:, k, lo:T], vcol("mu", m * KT + k), h1[:, k, lo:T],
                                           ALU.mult, ALU.add).then_inc(done, 1)
            return done, vector

        lo_ = es.enter_context(ExitStack())
        hid = lo_.enter_context(nc.sbuf_tensor("lora_hidden", [P, 2, T], F32))
        for m, (mu_i, name) in enumerate(((4, "w"), (5, "a"))):
            with ExitStack() as ph:
                mixed, f_mix = mix(ph, f"lora_{name}", mu_i, 0)
                w1 = ph.enter_context(nc.sbuf_tensor(f"lora_{name}1", [P, KT, P], F32))
                w_in, mm_done, out_done = sem(f"l1_in_{name}"), sem(f"l1_mm_{name}"), sem(f"l1_out_{name}")
                with nc.Block() as block:
                    @block.sync
                    def _(sp):
                        sp.dma_start(w1[:], A["w1" if m == 0 else "a1"]).then_inc(w_in, 16)

                    @block.vector
                    def _(v):
                        f_mix(v)

                    @block.tensor
                    def _(pe):
                        pe.wait_ge(w_in, 16)
                        for k in range(KT):
                            pe.wait_ge(mixed, k + 1)
                            for b, (a, n) in enumerate(BLK):
                                mm = pe.matmul(ps[:, b, 0:n], w1[:, k, :], xt[:, k, a:a + n], start=k == 0, stop=k == KT - 1)
                        mm.then_inc(mm_done, 1)

                    @block.scalar
                    def _(act):
                        act.wait_ge(mm_done, 1)
                        for b, (a, n) in enumerate(BLK):
                            act.activation(hid[:, m, a:a + n], ps[:, b, 0:n], ACT.Tanh if m == 0 else ACT.Copy).then_inc(out_done, 1)

        with ExitStack() as ph:
            w2 = ph.enter_context(nc.sbuf_tensor("lora_up", [P, 2, 2, NDIR, P], F32))
            sw = ph.enter_context(nc.sbuf_tensor("sw_out", [P, 2, NDIR, T], F32))
            sa = ph.enter_context(nc.sbuf_tensor("sa_out", [P, 2, NDIR, T], F32))
            w_in, st = [sem(f"l2_in{u}") for u in range(2)], [sem(f"l2_stored{u}") for u in range(2)]
            up_mm, up_out, zeroed = sem("l2_mm"), sem("l2_out"), sem("l2_zeroed")
            with nc.Block() as block:
                @block.sync
                def _(sp):
                    def load(u, j):
                        for d in range(NDIR):
                            r = slice(d * LORA, (d + 1) * LORA)
                            sp.dma_start(w2[r, u, :, d, :], A["w2a2"][j, r]).then_inc(w_in[u], 16)

                    def tile(u, j):
                        sp.wait_ge(up_out, j * 13 + 7)
                        for d in range(NDIR):
                            sp.dma_start(fe_v[j, :, FEATS.index("sw"), d], sw[:, u, d].rearrange("p (c t) -> p c t", t=CH)).then_inc(st[u], 16)
                        sp.wait_ge(up_out, j * 13 + 13)
                        sp.dma_start(sa_d[j], sa[:, u]).then_inc(st[u], 16)

                    sp.wait_ge(zeroed, 1)
                    for u in range(2):
                        load(u, u)
                    with sp.Fori(0, KT - 3, 2) as j:
                        for u in range(2):
                            tile(u, j + u)
                            load(u, j + (2 + u))
                    for u in range(2):
                        tile(u, KT - 2 + u)
                    for u in range(2):
                        sp.wait_ge(st[u], KT // 2 * 48)

                @block.vector
                def _(v):
                    v.memset(w2[:], 0.0).then_inc(zeroed, 1)

                @block.tensor
                def _(pe):
                    with pe.Fori(0, KT - 1, 2) as j:
                        for u in range(2):
                            pe.wait_ge(w_in[u], j * 16 + 32)
                            for q in range(4):
                                m, d = q // 2, q % 2
                                pe.wait_ge(up_out, (j + u) * 13 + (0, 0, 3, 7)[q])
                                for b, (a, n) in enumerate(BLK):
                                    mm = pe.matmul(ps[:, 3 * d + b, 0:n], w2[:, u, m, d, :], hid[:, m, a:a + n], start=True, stop=True)
                                mm.then_inc(up_mm, 1)

                @block.scalar
                def _(act):
                    with act.Fori(0, KT - 1, 2) as j:
                        for u in range(2):
                            act.wait_ge(st[u], j * 24)
                            for q in range(4):
                                m, d = q // 2, q % 2
                                act.wait_ge(up_mm, (j + u) * 4 + (q + 1))
                                n_out = 0
                                for b, (a, n) in enumerate(BLK):
                                    flip = m == 0 and d == 1
                                    pieces = [(x, y) for x, y in ((max(a, 0), min(a + n, CTX)), (max(a, CTX), min(a + n, T))) if y > x] if flip else [(a, a + n)]
                                    for x, y in pieces:
                                        out = (sw, sa)[m][:, u, d, x:y]
                                        if flip:
                                            lo, hi = (CTX - y, CTX - x) if y <= CTX else (CTX + T - y, CTX + T - x)
                                            out = sw[:, u, d, lo:hi][:, ::-1]
                                        act.activation(out, ps[:, 3 * d + b, x - a:y - a], ACT.Sigmoid,
                                                       bias=vec[:, bass.ds(j + (u + VEC[("w0", "a0")[m]][0] + d * KT), 1)]).then_inc(up_out, 1)
                                        n_out += 1
                                assert n_out == (3, 4, 3, 3)[q]
        lo_.close()

        LB = [(CTX, 512), (CTX + 512, 512)]
        with ExitStack() as ph:
            def sb(name, shape):
                return ph.enter_context(nc.sbuf_tensor(name, shape, F32))

            def chunks(t):
                return t.rearrange("p (c t) -> p c t", t=CH)

            w = sb("w_slab", [P, 2, KT, P])
            kn, sq = sb("k_nat", [P, 2, T]), sb("kk_sq", [P, 2, T])
            sa, am = sb("iclr", [P, NDIR, T]), sb("k_factor", [P, NDIR, T])
            fo = sb("k_feats", [P, 3, NDIR, T])
            ksum = sb("k_sum", [P, LAT])
            vo = (sq, am)
            ro = (fo[:, 1], fo[:, 2])
            rk, bv, ks, vn = fo[:, 0, 0, 0:LAT], fo[:, 0, 1, 0:LAT], kn[:, 0, 0:LAT], [sa[:, u, 0:LAT] for u in range(2)]
            go, gs = [sq[:, u, 0:LAT] for u in range(2)], [am[:, u, 0:LAT] for u in range(2)]

            w_in = [sem(f"w_in{u}") for u in range(2)]
            mixed, sa_in, k_mm, k_out, n_mm, root, am_ready, kk_steps, kd_steps, kd_st, kk_st = (sem(n) for n in (
                "mixed", "iclr_in", "k_mm", "k_out", "kk_norm_mm", "kk_root", "k_factor_ready", "kk_steps", "kd_steps", "kd_stored", "kk_stored"))
            v_mm, v_out, v_rev, v_st = sem("v_mm"), sem("v_out"), sem("v_reversed"), [sem(f"v_stored{u}") for u in range(2)]
            r_mm, kv_in, r_out, r_rev, rkc, b_mm, b_out, b_st, zr = (sem(n) for n in (
                "r_mm", "kv_in", "r_out", "r_reversed", "rk_ready", "b_mm", "b_out", "b_stored", "r_zero"))
            r_st = [sem(f"r_stored{u}") for u in range(2)]
            g_mm, g_sig, g_out, g_st = sem("g_mm"), sem("g_sig"), sem("g_out"), [sem(f"g_stored{u}") for u in range(2)]
            KK, KD = 11, 4
            pair = lambda t: t.rearrange("p (b t) -> p b t", b=2)
            parts = (slice(0, CTX), slice(CTX, T))

            with nc.Block() as block:
                @block.sync
                def _(sp):
                    def load_w(u, g):
                        sp.dma_start(w[:, u], A["rwin"][g]).then_inc(w_in[u], 16)

                    def k_store(j):
                        sp.wait_ge(kd_steps, j * KD + KD)
                        for d in range(NDIR):
                            sp.dma_start(fe_v[j, :, 0, d], chunks(fo[:, 0, d])).then_inc(kd_st, 16)
                        sp.dma_start(ks_d[j], ksum[:]).then_inc(kd_st, 16)
                        sp.wait_ge(kk_steps, j * KK + KK)
                        for f in (1, 2):
                            for d in range(NDIR):
                                sp.dma_start(fe_v[j, :, f, d], chunks(fo[:, f, d])).then_inc(kk_st, 16)

                    def load_sa(j):
                        sp.dma_start(sa[:], sa_d[j]).then_inc(sa_in, 16)

                    def k_tile(j, u):
                        sp.wait_ge(k_mm, j * 3)
                        load_w(1 - u, j + 1)
                        k_store(j - 1)
                        load_sa(j)

                    load_w(0, 0)
                    load_sa(0)
                    load_w(1, 1)
                    k_tile(1, 1)
                    with sp.Fori(2, KT - 1, 2) as j:
                        k_tile(j, 0)
                        k_tile(j + 1, 1)

                    def v_tile(j, u):
                        sp.wait_ge(v_mm, j * 3)
                        load_w(1 - u, j + (KT + 1))
                        sp.wait_ge(v_out, j * 3 + 3)
                        sp.wait_ge(v_rev, j * 2 + 2)
                        for d in range(NDIR):
                            sp.dma_start(fe_v[j, :, FEATS.index("v"), d], chunks(vo[u][:, d])).then_inc(v_st[u], 16)

                    sp.wait_ge(k_mm, KT * 3)
                    load_w(1, KT + 1)
                    k_store(KT - 1)
                    sp.wait_ge(v_out, 3)
                    sp.wait_ge(v_rev, 2)
                    for d in range(NDIR):
                        sp.dma_start(fe_v[0, :, FEATS.index("v"), d], chunks(vo[0][:, d])).then_inc(v_st[0], 16)
                    v_tile(1, 1)
                    with sp.Fori(2, KT - 1, 2) as j:
                        v_tile(j, 0)
                        v_tile(j + 1, 1)

                    def load_kv(j, u):
                        sp.dma_start(ks[:], ks_d[j]).then_inc(kv_in, 16)
                        sp.dma_start(chunks(vn[u]), fe_v[j, :, FEATS.index("v"), 0, 2:NCH]).then_inc(kv_in, 16)

                    def r_store(j, u):
                        sp.wait_ge(r_out, j * 2 + 2)
                        sp.wait_ge(r_rev, j * 2 + 2)
                        for d in range(NDIR):
                            sp.dma_start(fe_v[j, :, FEATS.index("r"), d], chunks(ro[u][:, d])).then_inc(r_st[u], 16)

                    def b_store(j):
                        sp.wait_ge(b_out, j + 1)
                        sp.dma_start(bv_d[j], bv).then_inc(b_st, 16)

                    def r_tile(j, u):
                        sp.wait_ge(r_mm, j * 2)
                        load_w(1 - u, j + (2 * KT + 1))
                        sp.wait_ge(rkc, j)
                        load_kv(j, u)
                        r_store(j, u)
                        b_store(j - 1)

                    sp.wait_ge(v_mm, KT * 3)
                    load_w(1, 2 * KT + 1)
                    sp.wait_ge(kd_st, KT * 48)
                    sp.wait_ge(kk_st, KT * 64)
                    for u in range(2):
                        sp.wait_ge(v_st[u], KT // 2 * 32)
                    load_kv(0, 0)
                    sp.wait_ge(zr, 2)
                    r_store(0, 0)
                    r_tile(1, 1)
                    with sp.Fori(2, KT - 1, 2) as j:
                        r_tile(j, 0)
                        r_tile(j + 1, 1)

                    def g_store(j, u):
                        sp.wait_ge(g_out, j * 2 + 2)
                        sp.dma_start(gz_d[j], go[u]).then_inc(g_st[u], 16)

                    def g_tile(j, u):
                        sp.wait_ge(g_mm, j * 2)
                        load_w(1 - u, j + (3 * KT + 1))
                        g_store(j, u)

                    sp.wait_ge(r_mm, KT * 2)
                    load_w(1, 3 * KT + 1)
                    b_store(KT - 1)
                    g_store(0, 0)
                    g_tile(1, 1)
                    with sp.Fori(2, KT - 3, 2) as j:
                        g_tile(j, 0)
                        g_tile(j + 1, 1)
                    g_tile(KT - 2, 0)
                    g_store(KT - 1, 1)
                    for u in range(2):
                        sp.wait_ge(r_st[u], KT // 2 * 32)
                        sp.wait_ge(g_st[u], KT // 2 * 16)
                    sp.wait_ge(b_st, KT * 16)

                @block.tensor
                def _(pe):
                    def project(m, j, u, mm_done, out_done, per_block, blks, first=False):
                        nb = len(blks)
                        pe.wait_ge(w_in[u], (j - u) * 8 + (m * (KT // 2) + 1) * 16)
                        if first:
                            for k in range(KT):
                                pe.wait_ge(mixed, m * KT + k + 1)
                                for b, (a, n) in enumerate(blks):
                                    mm = pe.matmul(ps[:, b, 0:n], w[:, u, k, :], xt[:, k, a:a + n], start=k == 0, stop=k == KT - 1)
                                    if k == KT - 1:
                                        mm.then_inc(mm_done, 1)
                            return
                        for b, (a, n) in enumerate(blks):
                            pe.wait_ge(out_done, (j - 1) * nb * per_block + (b + 1) * per_block)
                            for k in range(KT):
                                mm = pe.matmul(ps[:, b, 0:n], w[:, u, k, :], xt[:, k, a:a + n], start=k == 0, stop=k == KT - 1)
                            mm.then_inc(mm_done, 1)

                    def norm(j, u):
                        pe.wait_ge(k_out, j * 6 + 6)
                        if not isinstance(j, int) or j > 0:
                            pe.wait_ge(kk_steps, j * KK)
                        for b, (a, n) in enumerate(BLK):
                            mm = pe.matmul(ps[:, 3 + b, 0:n], hones[:], sq[:, u, a:a + n], start=True, stop=True)
                        mm.then_inc(n_mm, 1)

                    project(0, 0, 0, k_mm, k_out, 2, BLK, True)
                    project(0, 1, 1, k_mm, k_out, 2, BLK)
                    norm(0, 0)
                    with pe.Fori(2, KT - 1, 2) as j:
                        for u in range(2):
                            project(0, j + u, u, k_mm, k_out, 2, BLK)
                            norm(j + (u - 1), 1 - u)

                    pe.wait_ge(k_out, KT * 6)
                    project(1, 0, 0, v_mm, v_out, 1, BLK, True)
                    norm(KT - 1, 1)
                    project(1, 1, 1, v_mm, v_out, 1, BLK)
                    with pe.Fori(2, KT - 1, 2) as j:
                        for u in range(2):
                            project(1, j + u, u, v_mm, v_out, 1, BLK)

                    def bonus(j):
                        pe.wait_ge(rkc, j + 1)
                        if not isinstance(j, int) or j > 0:
                            pe.wait_ge(b_out, j)
                        for b in range(2):
                            mm = pe.matmul(ps[:, 3 + b, :], hones[:], rk[:, b * 512:(b + 1) * 512], start=True, stop=True)
                        mm.then_inc(b_mm, 1)

                    pe.wait_ge(v_out, KT * 3)
                    pe.wait_ge(kk_steps, KT * KK)
                    project(2, 0, 0, r_mm, r_out, 1, LB, True)
                    project(2, 1, 1, r_mm, r_out, 1, LB)
                    bonus(0)
                    with pe.Fori(2, KT - 1, 2) as j:
                        for u in range(2):
                            project(2, j + u, u, r_mm, r_out, 1, LB)
                            bonus(j + (u - 1))

                    pe.wait_ge(r_out, KT * 2)
                    project(3, 0, 0, g_mm, g_out, 1, LB, True)
                    bonus(KT - 1)
                    project(3, 1, 1, g_mm, g_out, 1, LB)
                    with pe.Fori(2, KT - 1, 2) as j:
                        for u in range(2):
                            project(3, j + u, u, g_mm, g_out, 1, LB)

                @block.scalar
                def _(act):
                    def norm_root(j):
                        act.wait_ge(n_mm, j + 1)
                        for p_ in (ps[:, 3:5, :], ps[:, 5, 0:256]):
                            act.activation(p_, p_, ACT.Sqrt).then_inc(root, 1)

                    def k_tile(j, u, first=False):
                        for b, (a, n) in enumerate(BLK):
                            act.wait_ge(k_mm, j * 3 + (b + 1))
                            if b == 0 and not first:
                                act.wait_ge(kk_steps, (j - 1) * KK)
                                act.wait_ge(kd_steps, (j - 1) * KD)
                            act.activation(kn[:, u, a:a + n], ps[:, b, 0:n], ACT.Copy).then_inc(k_out, 1)
                            act.activation(sq[:, u, a:a + n], ps[:, b, 0:n], ACT.Square, scale=vec[:, bass.ds(j + VEC["k_k"][0], 1)]).then_inc(k_out, 1)
                        if not first or u == 1:
                            norm_root(j - 1)
                        act.wait_ge(sa_in, j * 16 + 16)
                        if not first or u == 1:
                            act.wait_ge(kd_steps, j * KD)
                        for d in range(NDIR):
                            act.activation(am[:, d], sa[:, d], ACT.Identity, scale=vec[:, bass.ds(j + VEC["k_a"][0], 1)],
                                           bias=kam[:, bass.ds(j, 1)]).then_inc(am_ready, 1)

                    for u in range(2):
                        k_tile(u, u, True)
                    with act.Fori(2, KT - 1, 2) as j:
                        for u in range(2):
                            k_tile(j + u, u)

                    def v_tile(j, u, first=False):
                        for b, (a, n) in enumerate(BLK):
                            act.wait_ge(v_mm, j * 3 + (b + 1))
                            if b == 0 and not first:
                                act.wait_ge(v_st[u], (j - u) * 16)
                            act.activation(vo[u][:, 0, a:a + n], ps[:, b, 0:n], ACT.Copy).then_inc(v_out, 1)

                    norm_root(KT - 1)
                    v_tile(0, 0, True)
                    act.wait_ge(kd_steps, KT * KD)
                    v_tile(1, 1, True)
                    with act.Fori(2, KT - 1, 2) as j:
                        for u in range(2):
                            v_tile(j + u, u)

                    def r_tile(j, u, first=False):
                        for b, (a, n) in enumerate(LB):
                            act.wait_ge(r_mm, j * 2 + (b + 1))
                            if b == 0 and not first:
                                act.wait_ge(r_st[u], (j - u) * 16)
                            act.activation(ro[u][:, 0, a:a + n], ps[:, b, 0:n], ACT.Copy).then_inc(r_out, 1)

                    act.wait_ge(kk_st, KT * 64)
                    for u in range(2):
                        r_tile(u, u, True)
                    with act.Fori(2, KT - 1, 2) as j:
                        for u in range(2):
                            r_tile(j + u, u)

                    def g_tile(j, u, first=False):
                        for b in range(2):
                            act.wait_ge(g_mm, j * 2 + (b + 1))
                            if not first:
                                act.wait_ge(g_out, (j - 1) * 2)
                            act.activation(gs[u][:, b * 512:(b + 1) * 512], ps[:, b, :], ACT.Sigmoid).then_inc(g_sig, 1)

                    act.wait_ge(v_st[1], KT // 2 * 32)
                    for u in range(2):
                        g_tile(u, u, True)
                    with act.Fori(2, KT - 1, 2) as j:
                        for u in range(2):
                            g_tile(j + u, u)

                @block.gpsimd
                def _(g):
                    def k_tile(j, u):
                        step = 0
                        g.wait_ge(k_out, j * 6 + 6)
                        g.wait_ge(am_ready, j * 2 + 2)
                        g.wait_ge(kd_st, j * 48)
                        g.tensor_tensor(fo[:, 0, 0], kn[:, u], am[:, 0], ALU.mult).then_inc(kd_steps, 1)
                        for r in parts:
                            g.tensor_tensor(fo[:, 0, 1, r][:, ::-1], kn[:, u, r], am[:, 1, r], ALU.mult).then_inc(kd_steps, 1)
                        g.wait_ge(kd_steps, j * KD + 3)
                        g.tensor_tensor(ksum[:], fo[:, 0, 0, CTX:T], fo[:, 0, 1, CTX:T][:, ::-1], ALU.add).then_inc(kd_steps, 1)

                    with g.Fori(0, KT - 1, 2) as j:
                        for u in range(2):
                            k_tile(j + u, u)

                @block.vector
                def _(v):
                    def mix_in(m, mu_i, lo):
                        for k in range(KT):
                            v.scalar_tensor_tensor(xt[:, k, lo:T], dl[:, k, lo:T], vcol("mu", mu_i * KT + k), h1[:, k, lo:T],
                                                   ALU.mult, ALU.add).then_inc(mixed, 1)

                    def k_tile(j, u):
                        n = [0]

                        def count(ins):
                            n[0] += 1
                            ins.then_inc(kk_steps, 1)

                        banks = ((ps[:, 3:5, :], pair(kn[:, u, 0:1024]), pair(fo[:, 2, 0, 0:1024])),
                                 (ps[:, 5, 0:256], kn[:, u, 1024:T], fo[:, 2, 0, 1024:T]))
                        v.wait_ge(root, j * 2 + 2)
                        for p_, _, _ in banks:
                            count(v.tensor_scalar(p_, p_, 1e-12, None, ALU.max))
                        v.wait_ge(kk_steps, j * KK + 2)
                        for p_, _, _ in banks:
                            count(v.reciprocal(p_, p_))
                        v.wait_ge(kk_st, j * 64)
                        v.wait_ge(kk_steps, j * KK + 4)
                        for p_, k_, o in banks:
                            count(v.scalar_tensor_tensor(o, k_, nkk[:, bass.ds(j, 1)], p_, ALU.mult, ALU.mult))
                        v.wait_ge(sa_in, j * 16 + 16)
                        v.wait_ge(kk_steps, j * KK + 6)
                        count(v.scalar_tensor_tensor(fo[:, 1, 0], fo[:, 2, 0], -1.0, sa[:, 0], ALU.mult, ALU.mult))
                        for r in parts:
                            count(v.scalar_tensor_tensor(fo[:, 1, 1, r][:, ::-1], fo[:, 2, 0, r], -1.0, sa[:, 1, r], ALU.mult, ALU.mult))
                            count(v.tensor_copy(fo[:, 2, 1, r][:, ::-1], fo[:, 2, 0, r]))
                        assert n[0] == KK

                    mix_in(0, 1, 0)
                    with v.Fori(0, KT - 3, 2) as j:
                        for u in range(2):
                            k_tile(j + u, u)
                    v.wait_ge(k_mm, KT * 3)
                    mix_in(1, 2, 0)
                    k_tile(KT - 2, 0)
                    k_tile(KT - 1, 1)

                    def v_tile(j, u):
                        v.wait_ge(v_out, j * 3 + 3)
                        for r in parts:
                            v.tensor_copy(vo[u][:, 1, r][:, ::-1], vo[u][:, 0, r]).then_inc(v_rev, 1)

                    with v.Fori(0, KT - 3, 2) as j:
                        for u in range(2):
                            v_tile(j + u, u)
                    v_tile(KT - 2, 0)
                    v.wait_ge(v_mm, KT * 3)
                    mix_in(2, 0, CTX)
                    v_tile(KT - 1, 1)
                    v.wait_ge(kk_st, KT * 64)
                    v.wait_ge(kd_st, KT * 48)
                    for u in range(2):
                        v.memset(ro[u][:, :, 0:CTX], 0.0).then_inc(zr, 1)

                    def r_tile(j, u):
                        v.wait_ge(r_out, j * 2 + 2)
                        for a in (0, HALF):
                            v.tensor_copy(ro[u][:, 1, T - a - HALF:T - a][:, ::-1], ro[u][:, 0, CTX + a:CTX + a + HALF]).then_inc(r_rev, 1)

                    def bonus_out(j, u):
                        v.wait_ge(b_mm, j + 1)
                        v.wait_ge(b_st, j * 16)
                        v.tensor_tensor(pair(bv), ps[:, 3:5, :], pair(vn[u]), ALU.mult).then_inc(b_out, 1)

                    def rk_tile(j, u):
                        v.wait_ge(kv_in, j * 32 + 32)
                        v.scalar_tensor_tensor(rk, ro[u][:, 0, CTX:T], vec[:, bass.ds(j + VEC["r_k"][0], 1)], ks, ALU.mult, ALU.mult).then_inc(rkc, 1)

                    r_tile(0, 0)
                    rk_tile(0, 0)
                    with v.Fori(1, KT - 2, 2) as j:
                        for u in range(2):
                            r_tile(j + u, 1 - u)
                            bonus_out(j + (u - 1), u)
                            rk_tile(j + u, 1 - u)
                    v.wait_ge(r_mm, KT * 2)
                    mix_in(3, 3, CTX)
                    r_tile(KT - 1, 1)
                    bonus_out(KT - 2, 0)
                    rk_tile(KT - 1, 1)
                    bonus_out(KT - 1, 1)

                    def g_tile(j, u, first=False):
                        for b in range(2):
                            v.wait_ge(g_sig, j * 2 + (b + 1))
                            if b == 0 and not first:
                                v.wait_ge(g_st[u], (j - u) * 8)
                            v.tensor_tensor(go[u][:, b * 512:(b + 1) * 512], gs[u][:, b * 512:(b + 1) * 512], ps[:, b, :], ALU.mult).then_inc(g_out, 1)

                    v.wait_ge(v_st[0], KT // 2 * 32)
                    for u in range(2):
                        g_tile(u, u, True)
                    with v.Fori(2, KT - 1, 2) as j:
                        for u in range(2):
                            g_tile(j + u, u)

        l0.close()
        scan(nc, es, sem, ps, ident, eps, fe_d, y_d)

        fin = es.enter_context(ExitStack())
        gl = fin.enter_context(nc.sbuf_tensor("gated", [P, KT, LAT], F32))
        with ExitStack() as ph:
            def sb(name, shape):
                return ph.enter_context(nc.sbuf_tensor(name, shape, F32))
            yi, bi, gi = sb("y_in", [P, NDIR, LAT]), sb("bonus_in", [P, LAT]), sb("gate_in", [P, LAT])
            y, yc, sq, sd_ = (sb(n, [P, LAT]) for n in ("y", "y_centred", "y_sq", "y_std"))
            y_in, bg_in, chain, m_mm, sqr, v_mm, root = (sem("y_in"), sem("bg_in"), sem("y_chain"), sem("mean_mm"), sem("y_sq_ready"),
                                                        sem("var_mm"), sem("y_root"))
            NL = 9
            b2 = lambda t: t[:].rearrange("p (b t) -> p b t", b=2)
            with nc.Block() as block:
                @block.sync
                def _(sp):
                    with sp.Fori(0, KT) as j:
                        sp.wait_ge(chain, j * NL)
                        for d in range(NDIR):
                            sp.dma_start(yi[:, d].rearrange("p (c t) -> p c t", t=CH), y_v[j, :, d, 2:NCH]).then_inc(y_in, 16)
                        sp.dma_start(bi[:], bv_d[j]).then_inc(bg_in, 16)
                        sp.dma_start(gi[:], gz_d[j]).then_inc(bg_in, 16)

                @block.tensor
                def _(pe):
                    with pe.Fori(0, KT) as j:
                        pe.wait_ge(chain, j * NL + 1)
                        for b in range(2):
                            mm = pe.matmul(ps[:, b, :], hones[:], y[:, b * 512:(b + 1) * 512], start=True, stop=True)
                        mm.then_inc(m_mm, 1)
                        pe.wait_ge(sqr, j + 1)
                        for b in range(2):
                            mm = pe.matmul(ps[:, 2 + b, :], hones[:], sq[:, b * 512:(b + 1) * 512], start=True, stop=True)
                        mm.then_inc(v_mm, 1)

                @block.scalar
                def _(act):
                    with act.Fori(0, KT) as j:
                        act.wait_ge(chain, j * NL + 2)
                        act.activation(sq[:], yc[:], ACT.Square).then_inc(sqr, 1)
                        act.wait_ge(v_mm, j + 1)
                        act.activation(b2(sd_), ps[:, 2:4, :], ACT.Sqrt, scale=1.0 / HD, bias=eps[:, 1:2]).then_inc(root, 1)

                @block.vector
                def _(v):
                    with v.Fori(0, KT) as j:
                        n = [0]

                        def link(ins):
                            n[0] += 1
                            ins.then_inc(chain, 1)
                            v.wait_ge(chain, j * NL + n[0])

                        kv = lambda name: vec[:, bass.ds(j + VEC[name][0], 1)]
                        v.wait_ge(y_in, j * 32 + 32)
                        link(v.tensor_tensor(y[:], yi[:, 0], yi[:, 1][:, ::-1], ALU.add))
                        v.wait_ge(m_mm, j + 1)
                        link(v.scalar_tensor_tensor(b2(yc), ps[:, 0:2, :], -1.0 / HD, b2(y), ALU.mult, ALU.add))
                        v.wait_ge(root, j + 1)
                        link(v.reciprocal(sd_[:], sd_[:]))
                        link(v.tensor_tensor(yc[:], yc[:], sd_[:], ALU.mult))
                        link(v.tensor_scalar(yc[:], yc[:], kv("ln_w"), kv("ln_b"), ALU.mult, ALU.add))
                        v.wait_ge(bg_in, j * 32 + 32)
                        link(v.tensor_tensor(yc[:], yc[:], bi[:], ALU.add))
                        link(v.tensor_tensor(gl[:, j, :], yc[:], gi[:], ALU.mult))
                        link(v.tensor_copy(y[:, 0:1], y[:, 0:1]))
                        link(v.tensor_copy(y[:, 0:1], y[:, 0:1]))
                        assert n[0] == NL

        ol = fin.enter_context(nc.sbuf_tensor("o_last", [P, KT, LAT], F32))
        with ExitStack() as ph:
            out_proj(ph, "l1", A["rwout"], gl, ol, LAT)
        with ExitStack() as ph:
            rstd, rr, f_act, f_pe, f_dve = rms_stats(ph, "post1", lambda k: ol[:, k, :], LAT)
            x1 = ph.enter_context(nc.sbuf_tensor("x1", [P, KT, LAT], F32))
            x_in, on_ready, o_ready, st = sem("x1_in"), sem("on1_ready"), sem("out_ready"), sem("out_stored")
            with nc.Block() as block:
                @block.sync
                def _(sp):
                    sp.dma_start(x1[:], x1_d).then_inc(x_in, 16)
                    for k in range(KT):
                        sp.wait_ge(o_ready, k + 1)
                        sp.dma_start(A["out"][k], x1[:, k, :]).then_inc(st, 16)
                    sp.wait_ge(st, KT * 16)

                @block.scalar
                def _(act):
                    f_act(act, lambda e, k: None)

                @block.tensor
                def _(pe):
                    f_pe(pe)

                @block.vector
                def _(v):
                    f_dve(v)
                    v.wait_ge(x_in, 16)
                    for k in range(KT):
                        v.tensor_tensor(ol[:, k, :], ol[:, k, :], rstd[:], ALU.mult).then_inc(on_ready, 1)
                        v.wait_ge(on_ready, k + 1)
                        v.scalar_tensor_tensor(x1[:, k, :], ol[:, k, :], post_s[:, 1, k, 0:1], x1[:, k, :],
                                               ALU.mult, ALU.add).then_inc(o_ready, 1)


LEVELS = (2, 4, 8, 16, 32, 64)
BLOCKED = 16
GRAMS = ["at", "akt", "tok1", "tok2", "rbt", "rkt"]
DOUBLING = ["t2", "lv"]
for _k in LEVELS:
    DOUBLING += ([f"t{_k}"] if _k > 2 else []) + ([f"m{_k}"] if _k < 64 else []) + ([f"mt{_k}"] if _k > BLOCKED else [])
DOUBLING += ["wt"]
CHAIN = ["sa", "y", "st"]
STEPS = GRAMS + DOUBLING + CHAIN
NSTEP = len(STEPS)
EMPTIED = {n: "D" for n in STEPS + [f"mt{k}" for k in LEVELS]}
EMPTIED.update({n: "A" for n in ["at", "tok1", "tok2", "lv", "sa", "y", "mt64"] + [f"m{k}" for k in LEVELS if k < 64]})
BLOCK_STEPS = ("t32", "m32", "mt32", "t64", "mt64")
A_ORDER = [n for n in STEPS if EMPTIED[n] == "A"]
D_ORDER = [n for n in STEPS if EMPTIED[n] == "D"]
for _o in (A_ORDER, D_ORDER):
    for _n in ("t32", "m32", "mt32"):
        if _n in _o:
            _o.insert(_o.index(_n), _n + "_block0")
D_ORDER[D_ORDER.index("akt") + 1:1 + D_ORDER.index("akt")] = ["mt2_init", "m2_init"]
for _k in LEVELS:
    if _k <= BLOCKED:
        D_ORDER.insert(D_ORDER.index(f"t{_k * 2}" if _k < BLOCKED else "t32_block0"), f"mt{_k}")
D_ORDER.insert(D_ORDER.index("wt"), "wt_head0")
D_ORDER.insert(D_ORDER.index("st"), "st_head0")
D_ORDER += ["st_scaled_head0", "st_scaled"]


NS = 4
QUARTER = NSTEP // NS
AHEAD = [(NS - 1 - s) * QUARTER for s in range(NS)]
ORDER = [(s, STEPS[(t + AHEAD[s]) % NSTEP], (t + AHEAD[s]) // NSTEP) for t in range(NSTEP) for s in range(NS)]
ROTATED = [(s, STEPS[t - s * QUARTER], 0) for t in range(AHEAD[0]) for s in range(NS) if t >= s * QUARTER]
FINAL = [x for x in ORDER if x[2] == 0]


def vector_order(order):
    out, late = [], []
    for x in order:
        while late and (late[0][1] <= len(out) or late[0][0][0] == x[0]):
            out.append(late.pop(0)[0])
        out.append(x)
        s, name, ahead = x
        if name in [f"m{k}" for k in LEVELS if k <= BLOCKED]:
            late.append(((s, "mt" + name[1:], ahead), len(out) + 2))
    return out + [x for x, _ in late]


def scan(nc, es, sem, ps, ident, eps, fe_d, y_d):
    NIT = KT * NCH // NS
    U = 4
    ph = es.enter_context(ExitStack())

    def sb(name, shape, dt=F32):
        return ph.enter_context(nc.sbuf_tensor(name, shape, dt))

    two, streams = range(2), range(NS)
    feat = [sb(f"feat{s}", [P, NF, NDIR, CH]) for s in streams]
    kt, bt, at = ([feat[s][:, f] for s in streams] for f in range(3))
    cum = [sb(f"cum{s}", [P, NDIR, CH]) for s in streams]
    ex = [sb(f"exps{s}", [P, 3, NDIR, CH]) for s in streams]
    cumx = [ex[s][:, 1] for s in streams]
    pc, pcu = [sb(f"pend{s}", [P, NDIR]) for s in streams], [sb(f"pend_used{s}", [P, NDIR]) for s in streams]
    rt = [sb(f"rt{s}", [P, NDIR, CH]) for s in streams]
    btz, ktz, WTz = ([sb(f"{n}{s}", [P, 2, NDIR, CH]) for s in streams] for n in ("btz", "ktz", "WTz"))
    big = lambda n: [sb(f"{n}{s}", [P, U, CH]) for s in streams]
    AT, AKT, RBT, RKT, M2, MT2, M, MT, TOK1, TOK2, LV = (big(n) for n in ("AT", "AKT", "RBT", "RKT", "M2", "MT2", "M", "MT", "TOK1_", "TOK2_", "LV"))
    SA = LV
    TT = {k: big(f"TT{k}_") if k <= BLOCKED else M for k in LEVELS}
    Y = [sb(f"Y{s}", [P, NDIR, CH]) for s in streams]
    Sz, stmp = sb("Sz", [P, 2, NDIR, HD]), sb("S_sum", [P, NDIR, HD])
    hmask = sb("head_mask", [P, 2])
    keep = sb("keep", [P, NCH * (KT + 1)])
    restart = sb("restart", [P, NDIR * CH])
    ml = {k: sb(f"mask{k}", [P, CH], I32) for k in LEVELS if k <= BLOCKED}
    mt1 = sb("mask1t", [P, CH], I32)
    tick = sb("tick", [P, NS * len(D_ORDER)])
    mstrict, mincl = sb("mask_strict", [P, CH], I32), sb("mask_incl", [P, CH], I32)

    ld, cumr, cumxr, expr, xp, rtr, pes, evA, evD, yst = ([sem(f"{n}{s}") for s in streams] for n in (
        "feat_in", "cum_ready", "cumx_ready", "exp_ready", "operands_ready", "rt_ready", "step_done", "act_emptied", "dve_emptied", "y_stored"))
    init, msk = sem("scan_init"), sem("mask_ready")
    NA, ND = len(A_ORDER), len(D_ORDER)
    NB = 8 // NS
    NXP = 7

    def emptied(eng, s, it, name):
        if name in D_ORDER:
            eng.wait_ge(evD[s], it * ND + (D_ORDER.index(name) + 1))
        else:
            eng.wait_ge(evA[s], it * NA + (A_ORDER.index(name) + 1))

    def done(eng, s, it, name):
        eng.wait_ge(pes[s], it * NSTEP + (STEPS.index(name) + 1))

    def bank(s, name):
        return NB * s + STEPS.index(name) % NB

    def psv(s, name, n=CH):
        return ps[:, bank(s, name), 0:U * n].rearrange("p (u t) -> p u t", u=U)

    def changed(name):
        k = int(name.strip("mt"))
        r, c = (0, k) if name[:2] == "mt" else (k, 0)
        return [(slice(b + r, b + r + k), slice(b + c, b + c + k)) for b in range(0, CH, 2 * k)]

    def block_copies(s, name, t):
        k = int(name.strip("mt"))
        return [(t[s][rows, :, cols], ps[rows, bank(s, name), 0:U * k].rearrange("p (u t) -> p u t", u=U)) for rows, cols in changed(name)]

    bc = lambda m: m[:].unsqueeze(1).broadcast_to([P, U, CH])
    units = [(d, h) for d in range(NDIR) for h in range(2)]
    hp = lambda h: slice(h * HD, (h + 1) * HD)

    with nc.Block() as block:
        @block.gpsimd
        def _(g):
            n = [0]

            def link(ins):
                n[0] += 1
                ins.then_inc(msk, 1)
                g.wait_ge(msk, n[0])

            for k in ml:
                m = ml[k]
                link(g.memset(m[:], 1))
                v4 = m[:].rearrange("p (b e c) -> p b e c", e=2, c=k)
                link(g.memset(v4[:, :, 1, :], 0))
                v3 = m[:].rearrange("p (b q) -> p b q", q=2 * k)
                link(g.affine_select(out=v3, in_=v3, compare_op=ALU.is_ge, fill=0, base=-k, pattern=[[-2 * k, CH // (2 * k)], [0, 2 * k]], channel_multiplier=1))
                link(g.affine_select(out=v3, in_=v3, compare_op=ALU.is_ge, fill=0, base=2 * k - 1, pattern=[[2 * k, CH // (2 * k)], [0, 2 * k]], channel_multiplier=-1))
            link(g.memset(mt1[:], 1))
            v3 = mt1[:].rearrange("p (b e) -> p b e", e=2)
            link(g.memset(v3[:, :, 0], 0))
            for m in (1, -1):
                link(g.affine_select(out=v3, in_=v3, compare_op=ALU.is_ge, fill=0, base=0, pattern=[[-2 * m, CH // 2], [0, 2]], channel_multiplier=m))
            for m, base in ((mstrict, -1), (mincl, 0)):
                link(g.memset(m[:], 1))
                link(g.affine_select(out=m[:], in_=m[:], compare_op=ALU.is_ge, fill=0, base=base, pattern=[[1, CH]], channel_multiplier=-1))
            link(g.memset(keep[:], 1.0))
            link(g.memset(keep[:].rearrange("p (j c) -> p j c", c=NCH)[:, :, NCH - 1], 0.0))
            link(g.memset(restart[:], 1.0))
            link(g.memset(restart[:].rearrange("p (d t) -> p d t", d=NDIR)[:, :, 0], 0.0))
            link(g.memset(Sz[:], 0.0))
            link(g.memset(hmask[:], 0.0))
            for h in two:
                link(g.memset(hmask[hp(h), h:h + 1], 1.0))
            for s in streams:
                link(g.memset(WTz[s][:], 0.0))
                for z in (AKT[s], RBT[s], RKT[s]):
                    link(g.memset(z[:], 0.0))
                for e in [M2[s], MT2[s]] + [TT[k][s] for k in ml]:
                    for u in range(U):
                        g.tensor_copy(e[:, u, :], ident[:]).then_inc(init, 1)
            g.wait_ge(init, NS * U * (2 + len(ml)))

            def operands(s, n, it):
                g.wait_ge(cumr[s], n + 1)
                if it is not None:
                    g.wait_ge(expr[s], n * 4)
                g.tensor_tensor(cumx[s], cum[s][:], feat[s][:, 5], ALU.subtract).then_inc(cumxr[s], 1)
                g.wait_ge(expr[s], n * 4 + 4)
                if it is not None:
                    done(g, s, it, "rkt")
                for o, f, e in ((at, 2, 1), (bt, 1, 2), (kt, 0, 2)):
                    g.tensor_tensor(o[s], feat[s][:, f], ex[s][:, e], ALU.mult).then_inc(xp[s], 1)
                g.wait_ge(xp[s], n * NXP + 3)
                for o, oz in ((bt, btz), (kt, ktz)):
                    for h in two:
                        g.tensor_tensor(oz[s][:, h], o[s], hmask[:, h:h + 1].unsqueeze(1).broadcast_to([P, NDIR, CH]),
                                        ALU.mult).then_inc(xp[s], 1)

            for s in streams:
                operands(s, 0, None)
            with g.Fori(0, NIT - 1) as it:
                for s in streams:
                    operands(s, it + 1, it)

        @block.sync
        def _(sp):
            for s in streams:
                sp.dma_start(feat[s][:], fe_d[s]).then_inc(ld[s], 16)
            with sp.Fori(0, NIT - 1) as it:
                for s in streams:
                    done(sp, s, it, "rkt")
                    sp.dma_start(feat[s][:], fe_d[it * NS + (NS + s)]).then_inc(ld[s], 16)

        @block.scalar
        def _(act):
            def exps(s, n, first=False):
                act.wait_ge(cumr[s], n + 1)
                if not first:
                    act.wait_ge(xp[s], n * NXP)
                    act.wait_ge(rtr[s], n * 2)
                act.activation(ex[s][:, 0], cum[s][:], ACT.Exp, scale=-DECAY, bias=eps[:, 2:3]).then_inc(expr[s], 1)
                act.activation(ex[s][:, 2], cum[s][:], ACT.Exp, scale=DECAY, bias=eps[:, 3:4]).then_inc(expr[s], 1)
                act.activation(pc[s][:], cum[s][:, :, CH - 1], ACT.Exp, scale=-DECAY).then_inc(expr[s], 1)
                act.wait_ge(cumxr[s], n + 1)
                act.activation(ex[s][:, 1], cumx[s], ACT.Exp, scale=-DECAY, bias=eps[:, 2:3]).then_inc(expr[s], 1)

            for s in streams:
                exps(s, 0, True)
            dst = {"at": AT, "tok1": TOK1, "tok2": TOK2, "lv": LV, "sa": SA, "mt64": MT}
            dst.update({f"m{k}": M for k in LEVELS if k < 64})

            def empty(s, it, name):
                done(act, s, it, "mt32" if name == "m32" else name)
                if name == "y":
                    act.wait_ge(yst[s], it * 16)
                    act.activation(Y[s][:], ps[:, bank(s, name), 0:NDIR * CH].rearrange("p (d t) -> p d t", d=NDIR), ACT.Copy).then_inc(evA[s], 1)
                    emptied(act, s, it, "y")
                    act.dma_start(y_d[it * NS + s], Y[s][:]).then_inc(yst[s], 16)
                elif name in BLOCK_STEPS:
                    for n_, (o, i) in enumerate(block_copies(s, name, dst[name])):
                        act.activation(o, i, ACT.Copy).then_inc(evA[s], 1)
                else:
                    d = dst[name][s]
                    act.activation(d[:], psv(s, name), ACT.Copy).then_inc(evA[s], 1)

            def run(order, it, last=False):
                for s, name, ahead in order:
                    if EMPTIED[name] == "A":
                        empty(s, it + ahead, name)
                        if name == "mt64" and not last:
                            exps(s, it + 1)

            run(ROTATED, 0)
            with act.Fori(0, NIT - 1) as it:
                run(ORDER, it)
            run(FINAL, NIT - 1, True)
            for s in streams:
                act.wait_ge(yst[s], 16 * NIT)

        @block.vector
        def _(v):
            flat3 = lambda t: t[:].rearrange("p u t -> p (u t)")
            dst = {"akt": (AKT, mstrict), "rbt": (RBT, mincl), "rkt": (RKT, mincl)}
            dst.update({f"t{k}": (TT[k], ml[k]) for k in ml})

            def cumulate(s, n, first=False):
                v.wait_ge(ld[s], n * 16 + 16)
                if not first:
                    v.wait_ge(expr[s], n * 4)
                flat = lambda t: t.rearrange("p d t -> p (d t)")
                v.tensor_tensor_scan(flat(cum[s][:]), restart[:], flat(feat[s][:, 5]), 0.0, ALU.mult, ALU.add).then_inc(cumr[s], 1)

            def r_operand(s, n, it=None):
                v.wait_ge(expr[s], n * 4 + 4)
                if it is not None:
                    done(v, s, it, "y")
                v.tensor_tensor(rt[s][:], feat[s][:, 3], ex[s][:, 0], ALU.mult).then_inc(rtr[s], 1)
                v.tensor_scalar(pcu[s][:], pc[s][:], keep[:, bass.ds(n * NS + s, 1)], None, ALU.mult).then_inc(rtr[s], 1)

            def empty(s, it, name):
                if name == "mt2_init":
                    emptied(v, s, it, "at")
                    v.tensor_copy(tick[:, s * ND + D_ORDER.index(name):][:, 0:1], ident[:, 0:1])
                    v.copy_predicated(MT2[s][:], bc(mt1), AT[s][:]).then_inc(evD[s], 1)
                    return
                if name == "m2_init":
                    emptied(v, s, it, "mt2_init")
                    v.transpose(flat3(M2[s]), flat3(MT2[s])).then_inc(evD[s], 1)
                    return
                if name in [f"mt{k}" for k in LEVELS if k <= BLOCKED]:
                    emptied(v, s, it, "m" + name[2:])
                    v.transpose(flat3(MT[s]), flat3(M[s])).then_inc(evD[s], 1)
                    return
                done(v, s, it, name)
                if name == "t32":
                    emptied(v, s, it, "mt16")
                if name in BLOCK_STEPS:
                    for o, i in block_copies(s, name, MT if name[:2] == "mt" else TT[int(name[1:])]):
                        v.tensor_copy(o, i).then_inc(evD[s], 1)
                elif name in dst:
                    t, m = dst[name]
                    v.tensor_copy(tick[:, s * ND + D_ORDER.index(name):][:, 0:1], ident[:, 0:1])
                    v.copy_predicated(t[s][:], bc(m), psv(s, name)).then_inc(evD[s], 1)
                elif name == "wt":
                    o = ps[:, bank(s, name), 0:NDIR * CH].rearrange("p (d t) -> p d t", d=NDIR)
                    for h in two:
                        v.tensor_copy(WTz[s][hp(h), h], o[hp(h)]).then_inc(evD[s], 1)
                elif name == "st":
                    o = ps[:, bank(s, name), 0:NDIR * HD].rearrange("p (d t) -> p d t", d=NDIR)
                    for h in two:
                        v.tensor_tensor(stmp[hp(h)], Sz[hp(h), h], o[hp(h)], ALU.add).then_inc(evD[s], 1)
                    emptied(v, s, it, "st")
                    for h in two:
                        v.tensor_tensor(Sz[hp(h), h], stmp[hp(h)], pcu[s][hp(h)].unsqueeze(2).broadcast_to([HD, NDIR, HD]), ALU.mult).then_inc(evD[s], 1)
                    emptied(v, s, it, "st_scaled")
                else:
                    v.tensor_copy(MT[s][:], psv(s, name)).then_inc(evD[s], 1)

            v.wait_ge(init, NS * U * (2 + len(ml)))
            v.wait_ge(msk, 4 * len(ml) + 4 + 4 + 5 + 3 + NS * 4)
            for s in streams:
                cumulate(s, 0, True)
            for s in streams:
                r_operand(s, 0)

            def run(order, it, last=False):
                for s, name, ahead in order:
                    if EMPTIED[name] == "D":
                        empty(s, it + ahead, name)
                        if name == "akt":
                            empty(s, it + ahead, "mt2_init")
                            empty(s, it + ahead, "m2_init")
                        if name == "t64" and not last:
                            cumulate(s, it + 1)
                        if name == "st" and not last:
                            r_operand(s, it + 1, it)

            run(vector_order(ROTATED), 0)
            with v.Fori(0, NIT - 1) as it:
                run(vector_order(ORDER), it)
            run(vector_order(FINAL), NIT - 1, True)

        @block.tensor
        def _(pe):
            def bank_and_results(s, it, name, reads):
                i = STEPS.index(name)
                names = ([STEPS[i - NB]] if i >= NB else []) + list(reads)
                a = max([A_ORDER.index(x) + 1 for x in names if x in A_ORDER] + [0])
                d = max([D_ORDER.index(x) + 1 for x in names if x in D_ORDER] + [0])
                last = EMPTIED[STEPS[max(k for k in range(NSTEP) if k % NB == i)]] if i < NB else None
                if a or last == "A":
                    pe.wait_ge(evA[s], it * NA + a)
                if d or last == "D":
                    pe.wait_ge(evD[s], it * ND + d)

            def step(s, it, name, waits, mms):
                bank_and_results(s, it, name, waits)
                for out, l, r, st, sp_ in mms:
                    mm = pe.matmul(out, l, r, start=st, stop=sp_)
                mm.then_inc(pes[s], 1)

            def gram(s, it, name, L, R, waits=()):
                o = psv(s, name)
                step(s, it, name, waits, [(o[:, u, :], L[s][:, h, d, :], R[s][:, d], True, True) for u, (d, h) in enumerate(units)])

            def full(s, it, name, L, R, waits):
                o = psv(s, name)
                step(s, it, name, waits, [(o[:, u, :], L[s][:, u, :], R[s][:, u, :], True, True) for u in range(U)])

            def tr(s, it, name, pair):
                o = psv(s, name)
                bank_and_results(s, it, name, [])
                for q, src in enumerate(pair):
                    mm = pe.transpose(o[:, q, :], src, ident[:])
                mm.then_inc(pes[s], 1)

            def one(s, it, name):
                if name == "at":
                    pe.wait_ge(xp[s], it * NXP + NXP)
                    gram(s, it, name, btz, at)
                elif name == "akt":
                    gram(s, it, name, ktz, at)
                elif name == "tok1":
                    tr(s, it, name, [at[s][:, 0], at[s][:, 1], bt[s][:, 0], bt[s][:, 1]])
                elif name == "tok2":
                    tr(s, it, name, [kt[s][:, 0], kt[s][:, 1], feat[s][:, 4, 0], feat[s][:, 4, 1]])
                elif name == "rbt":
                    pe.wait_ge(rtr[s], it * 2 + 2)
                    gram(s, it, name, btz, rt)
                elif name == "rkt":
                    gram(s, it, name, ktz, rt)
                elif name == "t2":
                    full(s, it, name, AT, M2, ["at", "m2_init"])
                elif name == "m2":
                    full(s, it, name, MT2, TT[2], ["mt2_init", "t2"])
                elif name == "lv":
                    o = psv(s, name)
                    step(s, it, name, ["akt", "tok2"], [(o[:, u, :], AKT[s][:, u, :], TOK2[s][:, 2 + d, :], True, True) for u, (d, h) in enumerate(units)])
                elif name in BLOCK_STEPS:
                    k = int(name.strip("mt"))
                    L, R = {"t": (AT, M), "m": (MT, TT[k]), "mt": (TT[k], MT)}[name.rstrip("0123456789")]
                    reads = [f"m{k // 2}"] if name[0] == "t" else [f"mt{k // 2}", f"t{k}"]
                    mms = []
                    for rows, cols in changed(name):
                        o = ps[rows, bank(s, name), 0:U * k].rearrange("p (u t) -> p u t", u=U)
                        mms += [(o[:, u, :], L[s][:, u, rows], R[s][:, u, cols], True, True) for u in range(U)]
                    step(s, it, name, reads, mms)
                elif name[0] == "t":
                    k = int(name[1:])
                    full(s, it, name, AT, M, [f"m{k // 2}"])
                elif name[:2] == "mt":
                    k = int(name[2:])
                    full(s, it, name, TT[k], MT, [f"mt{k // 2}", f"t{k}"])
                elif name[0] == "m":
                    k = int(name[1:])
                    full(s, it, name, MT, TT[k], [f"mt{k // 2}", f"t{k}"])
                elif name == "wt":
                    o = ps[:, bank(s, name), 0:NDIR * CH].rearrange("p (d t) -> p d t", d=NDIR)
                    step(s, it, name, ["mt64", "tok1"], [(o[hp(h), d, :], TOK1[s][:, d, hp(h)], MT[s][:, u, :], True, True) for u, (d, h) in enumerate(units)])
                elif name == "sa":
                    o = psv(s, name)
                    mms = []
                    for u, (d, h) in enumerate(units):
                        mms += [(o[:, u, :], MT[s][:, u, :], LV[s][:, u, :], True, False),
                                (o[:, u, :].rearrange("p (h i) -> p h i", h=2), WTz[s][:, h, d, :], Sz[:, :, d, :], False, True)]
                    if s > 0:
                        emptied(pe, s - 1, it, "st_scaled")
                    elif not isinstance(it, int) or it > 0:
                        pe.wait_ge(evD[NS - 1], it * ND)
                    step(s, it, name, ["lv", "wt"], mms)
                elif name == "y":
                    o = ps[:, bank(s, name), 0:NDIR * CH].rearrange("p (d t) -> p d t", d=NDIR)
                    mms = []
                    for u, (d, h) in enumerate(units):
                        mms += [(o[hp(h), d, :], TOK2[s][:, 2 + d, hp(h)], RKT[s][:, u, :], True, False),
                                (o[hp(h), d, :], Sz[:, h, d, :], rt[s][:, d, :], False, False),
                                (o[hp(h), d, :], SA[s][:, u, hp(h)], RBT[s][:, u, :], False, True)]
                    step(s, it, name, ["sa", "rkt", "rbt"], mms)
                elif name == "st":
                    o = ps[:, bank(s, name), 0:NDIR * HD].rearrange("p (d t) -> p d t", d=NDIR)
                    mms = []
                    for u, (d, h) in enumerate(units):
                        mms += [(o[hp(h), d, :], TOK2[s][:, d, hp(h)], TOK2[s][:, 2 + d, hp(h)], True, False),
                                (o[hp(h), d, :], TOK1[s][:, 2 + d, hp(h)], SA[s][:, u, hp(h)], False, True)]
                    step(s, it, name, ["sa"], mms)

            pe.wait_ge(init, NS * U * (2 + len(ml)))
            for s, name, _ in ROTATED:
                one(s, 0, name)
            with pe.Fori(0, NIT - 1) as it:
                for s, name, ahead in ORDER:
                    one(s, it + ahead, name)
            for s, name, _ in FINAL:
                one(s, NIT - 1, name)
    ph.close()


def kernel(x, c, ctx, c_ctx, mod_w, mod_b, norm_pre, norm_post, f_w_in, f_w_mix, f_b_mix, f_w_out,
           r_mu, r_w_in, r_w0, r_w1, r_w2, r_a0, r_a1, r_a2, r_v0, r_v1, r_v2,
           r_k_k, r_k_a, r_r_k, r_ln_w, r_ln_b, r_w_out):
    import concourse.bacc as bacc
    from concourse.bass_utils import run_bass_kernel_spmd

    n = lambda a: np.asarray(a)
    cols = lambda a: n(a).reshape(-1, P).T
    slabs = lambda w, e: np.ascontiguousarray(n(w).reshape(KT, P, e, P).transpose(2, 1, 0, 3))
    vec = np.ascontiguousarray(np.concatenate([cols(a) for a in (
        c, c_ctx, n(mod_b)[0], n(mod_b)[1], norm_pre, norm_post, f_b_mix, r_mu, r_w0, r_a0, r_k_k, r_k_a, r_r_k, r_ln_w, r_ln_b)], axis=1))
    ang = lambda a, b, m: 2 * np.pi * ((np.outer(np.arange(a), np.arange(b)) % m) / m)
    cg = ang(P, P, P)
    ctab = np.stack([np.cos(cg), np.sin(cg)], axis=1) / np.sqrt(P)
    tg = ang(LAT, HALF, LAT).reshape(KT, P, HALF)
    tlat = np.stack([np.cos(tg), np.sin(tg)], axis=2).transpose(1, 0, 2, 3) / np.sqrt(LAT)
    alt = np.stack([(-1.0) ** np.arange(P)] * 2, axis=1) / np.sqrt(LAT)
    xg = ang(CTX, CTX, CTX).reshape(2, P, CTX)
    tctx = np.stack([np.cos(xg), -np.sin(xg)], axis=2).transpose(1, 0, 2, 3) / np.sqrt(CTX)
    f = lambda a: np.ascontiguousarray(a.astype(np.float32))
    up = lambda w: n(w).reshape(NDIR * LORA, KT, P).transpose(1, 0, 2)
    down = lambda w: np.ascontiguousarray(n(w).reshape(NDIR, KT, P, LORA).transpose(2, 1, 0, 3).reshape(P, KT, P))
    arrays = {
        "vec": vec,
        "xt": np.ascontiguousarray(np.concatenate([n(ctx)[0], n(x)[0]], axis=0).T.reshape(KT, P, T)),
        "modw": np.ascontiguousarray(n(mod_w).reshape(2, KT, P, 24, P).transpose(0, 3, 2, 1, 4).reshape(48, P, KT, P)),
        "fwin": slabs(n(f_w_in)[0], 2 * KT), "fwout": slabs(n(f_w_out)[0], KT), "rwout": slabs(n(r_w_out)[0], KT),
        "rwin": np.concatenate([slabs(n(r_w_in)[0, i], KT) for i in (1, 2, 0, 3)], axis=0),
        "wmix": np.ascontiguousarray(n(f_w_mix)[0].transpose(1, 0, 2)),
        "ctab": f(ctab), "tlat": f(tlat), "alt": f(alt), "tctx": f(tctx),
        "w1": down(n(r_w1)[0]), "a1": down(n(r_a1)[0]),
        "w2a2": np.ascontiguousarray(np.stack([up(n(r_w2)[0]), up(n(r_a2)[0])], axis=2)),
    }
    nc = bacc.Bacc("TRN2", target_bir_lowering=False, num_devices=1)
    A = {k: nc.dram_tensor(f"in_{k}", a.shape, F32, kind="ExternalInput").ap() for k, a in arrays.items()}
    A["out"] = nc.dram_tensor("out", [KT, P, LAT], F32, kind="ExternalOutput").ap()
    build(nc, A)
    r = run_bass_kernel_spmd(nc, [{f"in_{k}": a for k, a in arrays.items()}], core_ids=[0])
    return r.results[0]["out"].reshape(D, LAT).T[None]
```
